# Optimizing a Trainium2 kernel written in Bass

```python
import jax, jax.numpy as jnp
from jax import lax
import numpy as np
import math
import jax
import jax.numpy as jnp

D_MODEL = 1024
BATCH = 1
SEQ = 512
DEPTH = 1

CHUNK = 64
SGU_BLOCK = 128
D_A = 1024
A_GROUPS = 8
A_GROUP_DIM = D_A // A_GROUPS
D_B = 1024
POOL_WINDOWS = (2, 4, 8, 16)
B_GROUPS = len(POOL_WINDOWS)
B_GROUP_DIM = D_B // B_GROUPS
D_C = 1024
CONV_WIDTH = 3
N_BRANCH = 3
SPLIT_SIZES = (D_A, D_A, D_A, D_B, D_B, D_C, D_C, D_C, D_C, N_BRANCH * D_MODEL)
N_IN = sum(SPLIT_SIZES)
SPLIT_OFFSETS = tuple(int(o) for o in np.cumsum(SPLIT_SIZES)[:-1])
RMS_EPS = 1e-6
LN_EPS = 1e-5


def rmsnorm(x, g):
    xf = x.astype(jnp.float32)
    y = xf * lax.rsqrt(jnp.mean(xf * xf, axis=-1, keepdims=True) + RMS_EPS)
    return (y * g.astype(jnp.float32)).astype(x.dtype)

def layernorm(x, g, b):
    xf = x.astype(jnp.float32)
    mu = jnp.mean(xf, axis=-1, keepdims=True)
    var = jnp.mean(jnp.square(xf - mu), axis=-1, keepdims=True)
    y = (xf - mu) * lax.rsqrt(var + LN_EPS)
    return (y * g.astype(jnp.float32) + b.astype(jnp.float32)).astype(x.dtype)

def chunk_causal_mask():
    c = jnp.arange(SGU_BLOCK) // CHUNK
    return c[None, :] <= c[:, None]

def spatial_gating(u, v, w_s, b_s, ln_g, ln_b):
    bsz, s, _ = v.shape
    v = layernorm(v, ln_g, ln_b)
    vb = v.reshape(bsz, s // SGU_BLOCK, SGU_BLOCK, A_GROUPS, A_GROUP_DIM)
    w = jnp.where(chunk_causal_mask()[None], w_s, jnp.zeros_like(w_s))
    mixed = jnp.einsum('gij,bnjgc->bnigc', w, vb) + b_s.T[:, :, None]
    return u * mixed.reshape(bsz, s, D_A)

def multiscale_pool(p, w_g, b_g, scale):
    bsz, s, _ = p.shape
    pf = p.astype(jnp.float32)
    csum = jnp.cumsum(pf, axis=1)
    pos1 = jnp.arange(1, s + 1, dtype=jnp.int32)
    outs = []
    for k, win in enumerate(POOL_WINDOWS):
        sl = slice(k * B_GROUP_DIM, (k + 1) * B_GROUP_DIM)
        cg = csum[..., sl]
        shifted = jnp.pad(cg, ((0, 0), (win, 0), (0, 0)))[:, :s]
        count = jnp.minimum(pos1, win).astype(jnp.float32)[:, None]
        outs.append((cg - shifted) / count - pf[..., sl])
    d = jnp.concatenate(outs, axis=-1).astype(p.dtype)
    d = d.reshape(bsz, s, B_GROUPS, B_GROUP_DIM)
    y = jnp.einsum('bsgc,gcd->bsgd', d, w_g).reshape(bsz, s, D_B) + b_g
    return y * scale

def causal_depthwise_conv(h, w, b):
    s = h.shape[1]
    hp = jnp.pad(h, ((0, 0), (CONV_WIDTH - 1, 0), (0, 0)))
    y = sum(w[k] * hp[:, k:k + s] for k in range(CONV_WIDTH))
    return y + b

def first_inputs(seed: int = 0) -> dict:
    key = jax.random.key(seed)
    ks = jax.random.split(key, 20)

    def nrm(k, shape, scale):
        return jax.random.normal(k, shape, jnp.float32) * scale

    L = DEPTH
    return {
        "x": nrm(ks[0], (BATCH, SEQ, D_MODEL), 1.0),
        "norm_g": 1.0 + nrm(ks[1], (L, D_MODEL), 0.05),
        "w_in": nrm(ks[2], (L, D_MODEL, N_IN), D_MODEL ** -0.5),
        "sgu_ln_g": 1.0 + nrm(ks[3], (L, D_A), 0.05),
        "sgu_ln_b": nrm(ks[4], (L, D_A), 0.02),
        "sgu_w": nrm(ks[5], (L, A_GROUPS, SGU_BLOCK, SGU_BLOCK), SGU_BLOCK ** -0.5),
        "sgu_b": 1.0 + nrm(ks[6], (L, A_GROUPS, SGU_BLOCK), 0.05),
        "pool_w": nrm(ks[7], (L, B_GROUPS, B_GROUP_DIM, B_GROUP_DIM), B_GROUP_DIM ** -0.5),
        "pool_b": nrm(ks[8], (L, D_B), 0.01),
        "pool_scale": 1.0 + nrm(ks[9], (L, D_B), 0.1),
        "conv_w": nrm(ks[10], (L, CONV_WIDTH, D_C), CONV_WIDTH ** -0.5),
        "conv_b": nrm(ks[11], (L, D_C), 0.01),
        "w_branch_a": nrm(ks[12], (L, D_A, D_MODEL), D_A ** -0.5),
        "w_branch_b": nrm(ks[13], (L, D_B, D_MODEL), D_B ** -0.5),
        "w_branch_c": nrm(ks[14], (L, D_C, D_MODEL), D_C ** -0.5),
        "w_out": nrm(ks[15], (L, D_MODEL, D_MODEL), D_MODEL ** -0.5),
        "final_g": 1.0 + nrm(ks[16], (D_MODEL,), 0.05),
    }

def first_block(x, norm_g, w_in, sgu_ln_g, sgu_ln_b, sgu_w, sgu_b, pool_w, pool_b,
              pool_scale, conv_w, conv_b, w_branch_a, w_branch_b, w_branch_c,
              w_out, final_g):
    bsz, s, _ = x.shape
    for l in range(DEPTH):
        h = rmsnorm(x, norm_g[l])
        proj = jnp.einsum('bsd,dn->bsn', h, w_in[l])
        a_u, a_v, a_z, b_p, b_z, c_h, c_b, c_c, c_z, gate_logits = jnp.split(
            proj, SPLIT_OFFSETS, axis=-1)

        ya = spatial_gating(jax.nn.gelu(a_u), jax.nn.gelu(a_v), sgu_w[l], sgu_b[l],
                            sgu_ln_g[l], sgu_ln_b[l]) * jax.nn.silu(a_z)
        yb = multiscale_pool(b_p, pool_w[l], pool_b[l], pool_scale[l]) * jax.nn.silu(b_z)
        yc = c_b * causal_depthwise_conv(c_c * c_h, conv_w[l], conv_b[l]) * jax.nn.silu(c_z)

        gates = jax.nn.sigmoid(gate_logits.reshape(bsz, s, N_BRANCH, D_MODEL))
        merged = (gates[:, :, 0] * jnp.einsum('bsc,cd->bsd', ya, w_branch_a[l])
                  + gates[:, :, 1] * jnp.einsum('bsc,cd->bsd', yb, w_branch_b[l])
                  + gates[:, :, 2] * jnp.einsum('bsc,cd->bsd', yc, w_branch_c[l]))
        x = x + jnp.einsum('bsd,de->bse', merged, w_out[l])
    return rmsnorm(x, final_g)


N_MIXERS = 4
N_HEADS = 16
GROUP_HEADS = N_HEADS // N_MIXERS
HEAD_DIM = D_MODEL // N_HEADS
GROUP_WIDTH = GROUP_HEADS * HEAD_DIM

MOBA_BLOCK = 256
MOBA_TOPK = 3

NSA_KV_HEADS = 1
NSA_CMP_LEN = 32
NSA_CMP_STRIDE = 16
NSA_CMP_HIDDEN = 2 * HEAD_DIM
NSA_SEL_BLOCK = 64
NSA_SEL_TOPN = 16
NSA_WINDOW = 512

DIFF_QK_DIM = HEAD_DIM // 2

SWA_KV_HEADS = 2
SWA_WINDOW = 128

D_FF = 4 * D_MODEL

Q_BLOCK = 128
GATHER_Q_BLOCK = 32
NORM_EPS = 1e-6
NEG_INF = -1e30
TINY = 1e-30
FORCED_SCORE = 1e4

NSA_KV_WIDTH = NSA_KV_HEADS * HEAD_DIM
SWA_KV_WIDTH = SWA_KV_HEADS * HEAD_DIM
IN_SPLITS = (GROUP_WIDTH, GROUP_WIDTH, GROUP_WIDTH,
             GROUP_WIDTH, NSA_KV_WIDTH, NSA_KV_WIDTH, NSA_KV_WIDTH,
             NSA_KV_WIDTH, NSA_KV_WIDTH, NSA_KV_WIDTH, 3 * GROUP_HEADS,
             GROUP_WIDTH, GROUP_WIDTH, GROUP_WIDTH,
             GROUP_WIDTH, SWA_KV_WIDTH, SWA_KV_WIDTH)
D_IN = sum(IN_SPLITS)


def _rms_norm(x, gain):
    xf = x.astype(jnp.float32)
    y = xf * lax.rsqrt(jnp.mean(xf * xf, axis=-1, keepdims=True) + NORM_EPS)
    return (y * gain.astype(jnp.float32)).astype(x.dtype)

def _alibi_slopes(mixer):
    slopes = np.power(np.float32(2.0), np.arange(1, N_HEADS + 1, dtype=np.float32) * np.float32(-8.0 / N_HEADS))
    return jnp.asarray(slopes[mixer::N_MIXERS], dtype=jnp.float32)

def _masked_softmax(s, mask, sink=None):
    s = jnp.where(mask, s, NEG_INF)
    m = jnp.max(s, axis=-1, keepdims=True)
    if sink is not None:
        m = jnp.maximum(m, sink)
    p = jnp.where(mask, jnp.exp(s - m), 0.0)
    denom = jnp.sum(p, axis=-1, keepdims=True)
    if sink is not None:
        denom = denom + jnp.exp(sink - m)
    return p / jnp.maximum(denom, TINY)

def _heads(t, n):
    b, s, _ = t.shape
    return t.reshape(b, s, n, -1).transpose(0, 2, 1, 3)

def _merge(t):
    b, h, s, d = t.shape
    return t.transpose(0, 2, 1, 3).reshape(b, s, h * d)

def _to_chunks(t, qb, axis):
    shp = t.shape
    t = t.reshape(shp[:axis] + (shp[axis] // qb, qb) + shp[axis + 1:])
    return jnp.moveaxis(t, axis, 0)

def _from_chunks(t, axis):
    t = jnp.moveaxis(t, 0, axis)
    shp = t.shape
    return t.reshape(shp[:axis] + (shp[axis] * shp[axis + 1],) + shp[axis + 2:])

def _gather_blocks(blocks, idx):
    g = jax.vmap(jax.vmap(lambda bl, i: bl[i]))(blocks, idx)
    b, h, q, k, l, d = g.shape
    return g.reshape(b, h, q, k * l, d)

def _banded_attention(q, k, v, slopes, window, sinks=None):
    b, g, r, s, dh = q.shape
    nb = s // Q_BLOCK
    n_prev = -(-window // Q_BLOCK)

    def bands(t):
        tp = jnp.pad(t, ((0, 0), (0, 0), (n_prev * Q_BLOCK, 0), (0, 0))).reshape(b, g, nb + n_prev, Q_BLOCK, dh)
        return jnp.concatenate([tp[:, :, p:p + nb] for p in range(n_prev + 1)], axis=3)

    kb, vb = bands(k), bands(v)
    qpos = jnp.arange(s).reshape(nb, Q_BLOCK)
    kpos = (jnp.arange(nb)[:, None] - n_prev) * Q_BLOCK + jnp.arange((n_prev + 1) * Q_BLOCK)
    dist = qpos[:, :, None] - kpos[:, None, :]
    mask = (kpos[:, None, :] >= 0) & (dist >= 0) & (dist < window)
    qr = q.reshape(b, g, r, nb, Q_BLOCK, dh)
    sc = jnp.einsum('bgrnqd,bgnkd->bgrnqk', qr, kb).astype(jnp.float32) * (dh ** -0.5)
    sc = sc - slopes[:, :, None, None, None] * dist.astype(jnp.float32)
    sink = None if sinks is None else sinks.astype(jnp.float32)[:, :, None, None, None]
    p = _masked_softmax(sc, mask, sink)
    o = jnp.einsum('bgrnqk,bgnkd->bgrnqd', p.astype(vb.dtype), vb)
    return o.reshape(b, g, r, s, dh)

def _moba_attention(q, k, v, slopes):
    b, h, s, dh = q.shape
    nb = -(-s // MOBA_BLOCK)
    pad = nb * MOBA_BLOCK - s
    kp = jnp.pad(k, ((0, 0), (0, 0), (0, pad), (0, 0))).reshape(b, h, nb, MOBA_BLOCK, dh)
    vp = jnp.pad(v, ((0, 0), (0, 0), (0, pad), (0, 0))).reshape(b, h, nb, MOBA_BLOCK, dh)
    pos = jnp.arange(s)
    qblk = pos // MOBA_BLOCK
    own = jnp.broadcast_to(qblk[None, None, :, None], (b, h, s, 1))
    n_top = min(MOBA_TOPK, nb - 1)
    if n_top > 0:
        kmean = jnp.mean(kp.astype(jnp.float32), axis=3)
        gate = jnp.einsum('bhsd,bhnd->bhsn', q.astype(jnp.float32), kmean)
        past = jnp.arange(nb)[None, :] < qblk[:, None]
        gate = jnp.where(past, gate, NEG_INF)
        top_val, top_idx = lax.top_k(gate, n_top)
        sel_idx = jnp.concatenate([top_idx, own], axis=-1)
        sel_ok = jnp.concatenate([top_val > 0.5 * NEG_INF, jnp.ones(own.shape, dtype=bool)], axis=-1)
    else:
        sel_idx = own
        sel_ok = jnp.ones(own.shape, dtype=bool)
    scale = dh ** -0.5
    offs = jnp.arange(MOBA_BLOCK)

    def chunk(args):
        qc, ic, okc, tc = args
        kg = _gather_blocks(kp, ic)
        vg = _gather_blocks(vp, ic)
        kpos = (ic[..., None] * MOBA_BLOCK + offs).reshape(ic.shape[:3] + (-1,))
        ok = jnp.repeat(okc, MOBA_BLOCK, axis=-1)
        sc = jnp.einsum('bhqd,bhqkd->bhqk', qc, kg).astype(jnp.float32) * scale
        sc = sc - slopes[None, :, None, None] * (tc[:, None] - kpos).astype(jnp.float32)
        p = _masked_softmax(sc, ok & (kpos <= tc[:, None]))
        return jnp.einsum('bhqk,bhqkd->bhqd', p.astype(vg.dtype), vg)

    out = lax.map(chunk, (_to_chunks(q, GATHER_Q_BLOCK, 2), _to_chunks(sel_idx, GATHER_Q_BLOCK, 2),
                          _to_chunks(sel_ok, GATHER_Q_BLOCK, 2), pos.reshape(-1, GATHER_Q_BLOCK)))
    return _from_chunks(out, 2)

def _nsa_compress(x, pos_emb, w1, b1, w2):
    b, g, s, dh = x.shape
    n_sub = NSA_CMP_LEN // NSA_CMP_STRIDE
    c = x.reshape(b, g, s // NSA_CMP_STRIDE, NSA_CMP_STRIDE, dh)
    nc = c.shape[2] - n_sub + 1
    win = jnp.concatenate([c[:, :, i:i + nc] for i in range(n_sub)], axis=3)
    hid = jax.nn.gelu(jnp.einsum('bgnld,ldf->bgnf', win + pos_emb, w1) + b1)
    return jnp.einsum('bgnf,fd->bgnd', hid, w2)

def _cmp_to_sel_matrix(nc, nsel):
    cs = np.arange(nc)[:, None] * NSA_CMP_STRIDE
    bs = np.arange(nsel)[None, :] * NSA_SEL_BLOCK
    ov = np.clip(np.minimum(cs + NSA_CMP_LEN, bs + NSA_SEL_BLOCK) - np.maximum(cs, bs), 0, None)
    return (ov / NSA_CMP_LEN).astype(np.float32)

def _nsa_attention(q, k_cmp, v_cmp, k_slc, v_slc, k_win, v_win, gates, slopes, cmp_k, cmp_v):
    b, h, s, dh = q.shape
    g = NSA_KV_HEADS
    r = h // g
    qg = q.reshape(b, g, r, s, dh)
    sl = slopes.reshape(g, r)
    kc = _nsa_compress(k_cmp, *cmp_k)
    vc = _nsa_compress(v_cmp, *cmp_v)
    nc = kc.shape[2]
    cmp_end = jnp.arange(nc) * NSA_CMP_STRIDE + NSA_CMP_LEN - 1
    nsel = s // NSA_SEL_BLOCK
    n_top = min(NSA_SEL_TOPN, nsel)
    overlap = jnp.asarray(_cmp_to_sel_matrix(nc, nsel))
    ks = k_slc.reshape(b, g, nsel, NSA_SEL_BLOCK, dh)
    vs = v_slc.reshape(b, g, nsel, NSA_SEL_BLOCK, dh)
    blk_ids = jnp.arange(nsel)
    offs = jnp.arange(NSA_SEL_BLOCK)
    scale = dh ** -0.5

    def chunk(args):
        qc, tc = args
        sc = jnp.einsum('bgrqd,bgnd->bgrqn', qc, kc).astype(jnp.float32) * scale
        sc = sc - sl[:, :, None, None] * (tc[:, None] - cmp_end).astype(jnp.float32)
        p_c = _masked_softmax(sc, cmp_end <= tc[:, None])
        o_c = jnp.einsum('bgrqn,bgnd->bgrqd', p_c.astype(vc.dtype), vc)
        imp = jnp.einsum('bgrqn,ns->bgqs', p_c, overlap)
        qblk = tc // NSA_SEL_BLOCK
        forced = (blk_ids == 0) | (blk_ids == qblk[:, None]) | (blk_ids == qblk[:, None] - 1)
        score = jnp.where(forced, FORCED_SCORE, imp)
        score = jnp.where(blk_ids * NSA_SEL_BLOCK <= tc[:, None], score, NEG_INF)
        top_val, top_idx = lax.top_k(score, n_top)
        ok = jnp.repeat(top_val > 0.5 * NEG_INF, NSA_SEL_BLOCK, axis=-1)
        kg = _gather_blocks(ks, top_idx)
        vg = _gather_blocks(vs, top_idx)
        kpos = (top_idx[..., None] * NSA_SEL_BLOCK + offs).reshape(top_idx.shape[:3] + (-1,))
        dist = (tc[:, None] - kpos)[:, :, None]
        s2 = jnp.einsum('bgrqd,bgqkd->bgrqk', qc, kg).astype(jnp.float32) * scale
        s2 = s2 - sl[:, :, None, None] * dist.astype(jnp.float32)
        p_s = _masked_softmax(s2, ok[:, :, None] & (dist >= 0))
        o_s = jnp.einsum('bgrqk,bgqkd->bgrqd', p_s.astype(vg.dtype), vg)
        return o_c, o_s

    o_c, o_s = lax.map(chunk, (_to_chunks(qg, GATHER_Q_BLOCK, 3), jnp.arange(s).reshape(-1, GATHER_Q_BLOCK)))
    o_c = _from_chunks(o_c, 3).reshape(b, h, s, dh)
    o_s = _from_chunks(o_s, 3).reshape(b, h, s, dh)
    o_w = _banded_attention(qg, k_win, v_win, sl, NSA_WINDOW).reshape(b, h, s, dh)
    return gates[..., 0:1] * o_c + gates[..., 1:2] * o_s + gates[..., 2:3] * o_w

def _diff_attention(q1, q2, k1, k2, v, slopes, lq1, lk1, lq2, lk2, subln, lambda_init):
    b, h, s, dq = q1.shape
    scale = dq ** -0.5
    lam = (jnp.exp(jnp.sum(lq1.astype(jnp.float32) * lk1.astype(jnp.float32)))
           - jnp.exp(jnp.sum(lq2.astype(jnp.float32) * lk2.astype(jnp.float32))) + lambda_init)
    kpos = jnp.arange(s)

    def chunk(args):
        a1, a2, tc = args
        dist = (tc[:, None] - kpos).astype(jnp.float32)
        mask = dist >= 0
        bias = -slopes[:, None, None] * dist
        s1 = jnp.einsum('bhqd,bhkd->bhqk', a1, k1).astype(jnp.float32) * scale + bias
        s2 = jnp.einsum('bhqd,bhkd->bhqk', a2, k2).astype(jnp.float32) * scale + bias
        p = _masked_softmax(s1, mask) - lam * _masked_softmax(s2, mask)
        return jnp.einsum('bhqk,bhkd->bhqd', p.astype(v.dtype), v)

    o = lax.map(chunk, (_to_chunks(q1, Q_BLOCK, 2), _to_chunks(q2, Q_BLOCK, 2), kpos.reshape(-1, Q_BLOCK)))
    o = _from_chunks(o, 2)
    return _rms_norm(o, subln) * (1.0 - lambda_init)

def _swa_attention(q, k, v, slopes, sinks):
    b, h, s, dh = q.shape
    g = SWA_KV_HEADS
    r = h // g
    o = _banded_attention(q.reshape(b, g, r, s, dh), k, v, slopes.reshape(g, r), SWA_WINDOW, sinks.reshape(g, r))
    return o.reshape(b, h, s, dh)

def _conv_ffn(x, w_gate, w_up, conv_w, conv_b, w_down):
    a = x @ w_gate
    a = lax.conv_general_dilated(a, conv_w[:, None, :], window_strides=(1,), padding=[(CONV_WIDTH - 1, 0)],
                                 dimension_numbers=('NWC', 'WIO', 'NWC'), feature_group_count=a.shape[-1]) + conv_b
    return (jax.nn.gelu(a, approximate=True) * (x @ w_up)) @ w_down

def second_inputs(seed: int = 0) -> dict:
    key = jax.random.key(seed)
    keys = iter(jax.random.split(key, 40))

    def nrm(shape, scale):
        return jax.random.normal(next(keys), shape, jnp.float32) * scale

    L = DEPTH
    return {
        'x': nrm((BATCH, SEQ, D_MODEL), 1.0),
        'attn_pre_norm': 1.0 + nrm((L, D_MODEL), 0.02),
        'attn_post_norm': 1.0 + nrm((L, D_MODEL), 0.02),
        'ffn_pre_norm': 1.0 + nrm((L, D_MODEL), 0.02),
        'ffn_post_norm': 1.0 + nrm((L, D_MODEL), 0.02),
        'w_in': nrm((L, D_MODEL, D_IN), D_MODEL ** -0.5),
        'w_out': nrm((L, D_MODEL, D_MODEL), D_MODEL ** -0.5),
        'nsa_cmp_pos_k': nrm((L, NSA_CMP_LEN, HEAD_DIM), 0.1),
        'nsa_cmp_w1_k': nrm((L, NSA_CMP_LEN, HEAD_DIM, NSA_CMP_HIDDEN), (NSA_CMP_LEN * HEAD_DIM) ** -0.5),
        'nsa_cmp_b1_k': nrm((L, NSA_CMP_HIDDEN), 0.01),
        'nsa_cmp_w2_k': nrm((L, NSA_CMP_HIDDEN, HEAD_DIM), NSA_CMP_HIDDEN ** -0.5),
        'nsa_cmp_pos_v': nrm((L, NSA_CMP_LEN, HEAD_DIM), 0.1),
        'nsa_cmp_w1_v': nrm((L, NSA_CMP_LEN, HEAD_DIM, NSA_CMP_HIDDEN), (NSA_CMP_LEN * HEAD_DIM) ** -0.5),
        'nsa_cmp_b1_v': nrm((L, NSA_CMP_HIDDEN), 0.01),
        'nsa_cmp_w2_v': nrm((L, NSA_CMP_HIDDEN, HEAD_DIM), NSA_CMP_HIDDEN ** -0.5),
        'diff_lambda_q1': nrm((L, DIFF_QK_DIM), 0.1),
        'diff_lambda_k1': nrm((L, DIFF_QK_DIM), 0.1),
        'diff_lambda_q2': nrm((L, DIFF_QK_DIM), 0.1),
        'diff_lambda_k2': nrm((L, DIFF_QK_DIM), 0.1),
        'diff_subln': 1.0 + nrm((L, HEAD_DIM), 0.02),
        'swa_sinks': nrm((L, GROUP_HEADS), 0.5),
        'ffn_w_gate': nrm((L, D_MODEL, D_FF), D_MODEL ** -0.5),
        'ffn_w_up': nrm((L, D_MODEL, D_FF), D_MODEL ** -0.5),
        'ffn_conv_w': nrm((L, CONV_WIDTH, D_FF), CONV_WIDTH ** -0.5),
        'ffn_conv_b': nrm((L, D_FF), 0.01),
        'ffn_w_down': nrm((L, D_FF, D_MODEL), D_FF ** -0.5),
    }

def second_block(x, attn_pre_norm, attn_post_norm, ffn_pre_norm, ffn_post_norm, w_in, w_out,
              nsa_cmp_pos_k, nsa_cmp_w1_k, nsa_cmp_b1_k, nsa_cmp_w2_k,
              nsa_cmp_pos_v, nsa_cmp_w1_v, nsa_cmp_b1_v, nsa_cmp_w2_v,
              diff_lambda_q1, diff_lambda_k1, diff_lambda_q2, diff_lambda_k2, diff_subln,
              swa_sinks, ffn_w_gate, ffn_w_up, ffn_conv_w, ffn_conv_b, ffn_w_down):
    b, s, _ = x.shape
    splits = np.cumsum(IN_SPLITS)[:-1].tolist()
    for l in range(DEPTH):
        h = _rms_norm(x, attn_pre_norm[l])
        (mq, mk, mv, nq, nkc, nvc, nks, nvs, nkw, nvw, ngate,
         dq, dk, dv, sq, sk, sv) = jnp.split(h @ w_in[l], splits, axis=-1)
        o_moba = _moba_attention(_heads(mq, GROUP_HEADS), _heads(mk, GROUP_HEADS), _heads(mv, GROUP_HEADS),
                                 _alibi_slopes(0))
        gates = jax.nn.sigmoid(ngate.reshape(b, s, GROUP_HEADS, 3).transpose(0, 2, 1, 3))
        o_nsa = _nsa_attention(_heads(nq, GROUP_HEADS), _heads(nkc, NSA_KV_HEADS), _heads(nvc, NSA_KV_HEADS),
                               _heads(nks, NSA_KV_HEADS), _heads(nvs, NSA_KV_HEADS),
                               _heads(nkw, NSA_KV_HEADS), _heads(nvw, NSA_KV_HEADS), gates, _alibi_slopes(1),
                               (nsa_cmp_pos_k[l], nsa_cmp_w1_k[l], nsa_cmp_b1_k[l], nsa_cmp_w2_k[l]),
                               (nsa_cmp_pos_v[l], nsa_cmp_w1_v[l], nsa_cmp_b1_v[l], nsa_cmp_w2_v[l]))
        dq4 = _heads(dq, GROUP_HEADS)
        dk4 = _heads(dk, GROUP_HEADS)
        lambda_init = 0.8 - 0.6 * math.exp(-0.3 * l)
        o_diff = _diff_attention(dq4[..., :DIFF_QK_DIM], dq4[..., DIFF_QK_DIM:],
                                 dk4[..., :DIFF_QK_DIM], dk4[..., DIFF_QK_DIM:], _heads(dv, GROUP_HEADS),
                                 _alibi_slopes(2), diff_lambda_q1[l], diff_lambda_k1[l],
                                 diff_lambda_q2[l], diff_lambda_k2[l], diff_subln[l], lambda_init)
        o_swa = _swa_attention(_heads(sq, GROUP_HEADS), _heads(sk, SWA_KV_HEADS), _heads(sv, SWA_KV_HEADS),
                               _alibi_slopes(3), swa_sinks[l])
        mix = jnp.concatenate([_merge(o_moba), _merge(o_nsa), _merge(o_diff), _merge(o_swa)], axis=-1)
        x = x + _rms_norm(mix @ w_out[l], attn_post_norm[l])
        h = _rms_norm(x, ffn_pre_norm[l])
        x = x + _rms_norm(_conv_ffn(h, ffn_w_gate[l], ffn_w_up[l], ffn_conv_w[l], ffn_conv_b[l], ffn_w_down[l]),
                          ffn_post_norm[l])
    return x


def setup_inputs(seed=0):
    out = dict(first_inputs(seed))
    for name, value in second_inputs(seed + 1).items():
        if name != "x":
            out[name + "_2"] = value
    return out


def reference(
    x, norm_g, w_in, sgu_ln_g, sgu_ln_b, sgu_w, sgu_b, pool_w, pool_b, pool_scale, conv_w,
    conv_b, w_branch_a, w_branch_b, w_branch_c, w_out, final_g, attn_pre_norm_2,
    attn_post_norm_2, ffn_pre_norm_2, ffn_post_norm_2, w_in_2, w_out_2, nsa_cmp_pos_k_2,
    nsa_cmp_w1_k_2, nsa_cmp_b1_k_2, nsa_cmp_w2_k_2, nsa_cmp_pos_v_2, nsa_cmp_w1_v_2,
    nsa_cmp_b1_v_2, nsa_cmp_w2_v_2, diff_lambda_q1_2, diff_lambda_k1_2, diff_lambda_q2_2,
    diff_lambda_k2_2, diff_subln_2, swa_sinks_2, ffn_w_gate_2, ffn_w_up_2, ffn_conv_w_2,
    ffn_conv_b_2, ffn_w_down_2,
):
    x = first_block(
        x, norm_g, w_in, sgu_ln_g, sgu_ln_b, sgu_w, sgu_b, pool_w, pool_b, pool_scale, conv_w,
        conv_b, w_branch_a, w_branch_b, w_branch_c, w_out, final_g,
    )
    return second_block(
        x, attn_pre_norm_2, attn_post_norm_2, ffn_pre_norm_2, ffn_post_norm_2, w_in_2, w_out_2,
        nsa_cmp_pos_k_2, nsa_cmp_w1_k_2, nsa_cmp_b1_k_2, nsa_cmp_w2_k_2, nsa_cmp_pos_v_2,
        nsa_cmp_w1_v_2, nsa_cmp_b1_v_2, nsa_cmp_w2_v_2, diff_lambda_q1_2, diff_lambda_k1_2,
        diff_lambda_q2_2, diff_lambda_k2_2, diff_subln_2, swa_sinks_2, ffn_w_gate_2, ffn_w_up_2,
        ffn_conv_w_2, ffn_conv_b_2, ffn_w_down_2,
    )


_drawn_inputs = setup_inputs


def setup_inputs(seed=0):
    import zlib

    import numpy as np

    out = dict(_drawn_inputs(seed))
    spreads = {}
    factors = {'sgu_ln_g': 4.755,
     'sgu_ln_b': 8.0,
     'sgu_b': 3.822,
     'pool_b': 8.0,
     'conv_b': 8.0,
     'attn_post_norm_2': 3.481,
     'ffn_pre_norm_2': 3.417,
     'ffn_post_norm_2': 52.62,
     'nsa_cmp_pos_k_2': 54.307,
     'nsa_cmp_b1_k_2': 200.0,
     'nsa_cmp_b1_v_2': 45.42,
     'diff_lambda_q1_2': 6.078,
     'diff_lambda_k1_2': 3.14,
     'diff_lambda_q2_2': 6.674,
     'diff_lambda_k2_2': 4.535,
     'diff_subln_2': 4.536,
     'swa_sinks_2': 129.416,
     'ffn_conv_b_2': 24.288,
     'nsa_cmp_w1_k_2': 3.253,
     'nsa_cmp_w2_k_2': 3.5,
     'nsa_cmp_pos_v_2': 5.761}
    for name, (base, spread) in spreads.items():
        noise = np.random.default_rng([zlib.crc32(name.encode()), seed]).standard_normal(out[name].shape)
        drawn = base * np.exp(spread * noise) if base else spread * noise
        out[name] = jnp.asarray(drawn.astype(out[name].dtype))
    for name, factor in factors.items():
        out[name] = (out[name] * factor).astype(out[name].dtype)
    return out
```

```python
from contextlib import ExitStack

import numpy as np
import concourse.bass as bass
from concourse import mybir

F32 = mybir.dt.float32
F32R = mybir.dt.float32r
ALU = mybir.AluOpType
ACT = mybir.ActivationFunctionType
AX = mybir.AxisListType
ds = bass.ds

P = 128
S = 512
D = 1024
MT = S // P
KT = D // P
CHUNK = 64
SGU_GROUPS = 8
POOL_WINDOWS = (2, 4, 8, 16)
PAD = 16
TAPS = 3
HEADS = 4
DH = 64
DQ = DH // 2
N_CMP = S // 16 - 1
CMP_LEN = 32
CMP_HID = 2 * DH
SWA_WINDOW = 128
FF = 4 * D
FCH = 4
RMS_EPS, LN_EPS = 1e-6, 1e-5
LAMBDA_INIT = 0.2
TINY = 1e-30
SLAB = 2048

(A_U, A_V, A_Z, B_P, B_Z, C_H, C_B, C_C, C_Z, GATES) = (D * i for i in range(10))
_W2 = np.cumsum([0, 256, 256, 256, 256, 64, 64, 64, 64, 64, 64, 12, 256, 256, 256, 256, 128, 128])
(MQ, MK, MV, NQ, NKC, NVC, NKS, NVS, NKW, NVW, NGATE, DQ_, DK_, DV, SQ, SK, SV, _END) = map(int, _W2)
G_NORM, G_POOLB, G_POOLS, G_CONVW, G_CONVB, G_ATTN, G_FFN, G_FCW, G_FCB, G_END = (
    0, 8, 16, 24, 48, 56, 64, 72, 168, 200)

class Track:

    def __init__(self, sem, steps, rounds=1):
        self.sem, self.steps, self.rounds, self.pos = sem, list(steps), rounds, 0
        assert len(set(self.steps)) == len(self.steps)

    def at(self, name, i=0):
        return self.sem, (i + 1) * len(self.steps) + self.steps.index(name) + 1

    def before(self, name, i=0):
        return self.sem, i * len(self.steps) + self.steps.index(name) + 1

    def end(self):
        return self.sem, (self.rounds + 1) * len(self.steps)

    def done(self, ins, name):
        assert self.steps[self.pos % len(self.steps)] == name, (name, self.steps[self.pos % len(self.steps)])
        self.pos += 1
        ins.then_inc(self.sem, 1)

def stand(e, gate):
    e.sem_inc(gate, 1)

def step(e, track, name, waits, make, gate=None):
    for w in waits:
        e.wait_ge(*w)
    if gate is not None:
        stand(e, gate)
    track.done(make(), name)

def build(nc, T, out):
    with ExitStack() as ctx:
        def sem(name):
            return ctx.enter_context(nc.semaphore(name))

        def sb(name, shape, dt=F32, stack=ctx):
            return stack.enter_context(nc.sbuf_tensor(name, shape, dt))

        x_res = sb("x_res", [P, MT, D])
        hT = [sb("hT_hi", [P, KT, S], F32R), sb("hT_lo", [P, KT, S], F32R)]
        raw = [sb(f"raw{s}", [P, SLAB]) for s in range(2)]
        w_hi = [sb(f"w_hi{s}", [P, SLAB], F32R) for s in range(2)]
        w_lo = [sb(f"w_lo{s}", [P, SLAB], F32R) for s in range(2)]
        ident = sb("ident", [P, P])
        gains = sb("gains", [P, G_END])
        stat = sb("stat", [P, 64])
        rowA = sb("rowA", [P, D])
        rowB = sb("rowB", [P, D])
        rowC = sb("rowC", [P, D])
        junk = sb("junk", [P, 1])
        tU = sb("tU", [P, 2, S])
        tZ = sb("tZ", [P, 2, S])
        tY = sb("tY", [P, 2, S])
        padded = sb("padded", [P, 2, PAD + S])
        psum = ctx.enter_context(nc.psum_tensor("psum", [P, 8, S], F32))
        bank = [psum[:, b, :] for b in range(8)]
        pair = [psum[:, 2 * q:2 * q + 2, :] for q in range(4)]

        one = ExitStack()
        yT = [sb("yT_hi", [P, KT, S], F32R, one), sb("yT_lo", [P, KT, S], F32R, one)]
        v_tok = sb("v_tok", [P, MT, D], stack=one)
        pool_w = sb("pool_w_sb", [P, 2, 4, 256], stack=one)
        winA = sb("winA", [P, 2, PAD + S], stack=one)
        winB = sb("winB", [P, 2, PAD + S], stack=one)
        dT = sb("dT", [P, 2, S], stack=one)
        sgu_w = sb("sgu_w_sb", [P, SGU_GROUPS, P], stack=one)
        wT = sb("wT", [P, SGU_GROUPS, P], stack=one)
        rows = sb("rows", [P, 2, P], stack=one)
        ratio = sb("ratio_sb", [P, 4, PAD], stack=one)
        one.close()
        merged = v_tok[:, :, :].rearrange("p m (a s) -> p (m a) s", s=S)

        program = ExitStack()
        blk = program.enter_context(nc.Block())
        engines = {"sync": blk.sync, "tensor": blk.tensor, "scalar": blk.scalar,
                   "vector": blk.vector, "gpsimd": blk.gpsimd}

        def on(engine):
            return engines[engine]

        s_raw = [sem("raw_full0"), sem("raw_full1")]
        s_hi = sem("hi_done")
        s_lo = sem("lo_done")
        s_used = sem("slab_used")
        s_gate = sem("gate")
        s_x = [sem(f"x_in{m}") for m in range(MT)]
        s_const = sem("const_in")
        s_row = sem("rows_in")
        s_att = sem("attention_in")
        s_out = sem("out_stored")

        def used(h, slot):
            return s_used, 2 * h + slot + 3

        def snapped(i):
            return i if isinstance(i, int) else nc.sync.snap(i)

        def load(e, h, slot, pieces):
            e.wait_ge(s_lo, 2 * h + slot + 1)
            assert len(pieces) == 2
            for to, src in pieces:
                e.dma_start(to, src).then_inc(s_raw[slot], 16)

        def split_hi(e, h, slot):
            e.wait_ge(s_raw[slot], 32 * (h + 1))
            e.wait_ge(s_used, 2 * h + slot + 1)
            e.activation(w_hi[slot][:, :], raw[slot][:, :], ACT.Copy).then_inc(s_hi, 1)

        def split_lo(e, h, slot):
            e.wait_ge(s_hi, 2 * h + slot + 1)
            e.tensor_tensor(w_lo[slot][:, :], raw[slot][:, :], w_hi[slot][:, :].bitcast(F32),
                            ALU.subtract).then_inc(s_lo, 1)

        def after(h, slot):
            return (h, 1) if slot == 0 else (h + 1, 0)

        def t_pieces(slot, w, col):
            col = snapped(col)
            to = raw[slot][:, :].rearrange("p (k c) -> p k c", k=KT)
            src = w.rearrange("(k p) c -> p k c", p=P)
            return [(to[:, q:q + 4, :], src[:, q:q + 4, ds(col, 256)]) for q in (4, 0)]

        def n_pieces(slot, w, row, col):
            row, col = snapped(row), snapped(col)
            to = raw[slot][:, :].rearrange("p (k c) -> p k c", k=4)
            src = w.rearrange("(k p) c -> p k c", p=P)
            return [(to[:, q:q + 2, :], src[:, ds(row + q, 2), ds(col, 512)]) for q in (2, 0)]

        def product(e, to, stat_hi, stat_lo, mov_hi, mov_lo, first, last):
            e.matmul(to, stat_lo, mov_hi, start=first, stop=False)
            e.matmul(to, stat_hi, mov_lo, start=False, stop=False)
            return e.matmul(to, stat_hi, mov_hi, start=False, stop=last)

        def split_ready(e, h, slot):
            e.wait_ge(s_hi, 2 * h + slot + 1)
            e.wait_ge(s_lo, 2 * h + slot + 3)

        def gemm_t(e, h, slot, act, banks, waits):
            split_ready(e, h, slot)
            for w in waits:
                e.wait_ge(*w)
            hi = w_hi[slot][:, :].rearrange("p (k c) -> p k c", k=KT)
            lo = w_lo[slot][:, :].rearrange("p (k c) -> p k c", k=KT)
            for t in range(2):
                for k in range(KT):
                    c = slice(P * t, P * t + P)
                    last = product(e, bank[banks[t]], hi[:, k, c], lo[:, k, c],
                                   act[0][:, k, :], act[1][:, k, :], k == 0, k == KT - 1)
            last.then_inc(s_used, 1)

        def gemm_n(e, h, act, banks, free, track, width=512):
            for half in range(2):
                split_ready(e, h, half)
                hi = w_hi[half][:, :].rearrange("p (k c) -> p k c", k=4)
                lo = w_lo[half][:, :].rearrange("p (k c) -> p k c", k=4)
                for m in range(MT):
                    if half == 0:
                        e.wait_ge(*free(m))
                    for k in range(4):
                        kk, tok = 4 * half + k, slice(P * m, P * m + P)
                        last = product(e, bank[banks[m]][:, 0:width], act[0][:, kk, tok], act[1][:, kk, tok],
                                       hi[:, k, 0:width], lo[:, k, 0:width], kk == 0, kk == KT - 1)
                    if half == 1 and m < MT - 1:
                        track.done(last, f"m{m}")
                last.then_inc(s_used, 1)

        def n_ready(m, track, i, h):
            return track.at(f"m{m}", i) if m < MT - 1 else used(h, 1)

        state = {"prev": [], "n": 0}

        def phase(name, act=(), dve=(), pe=(), pool=(), rounds=1, before_entry=None):
            tr = {}
            for eng, steps in (("scalar", act), ("vector", dve), ("tensor", pe), ("gpsimd", pool)):
                tr[eng] = Track(sem(f"{name}_{eng}"), steps, rounds) if steps else None
            prev = [t for t in state["prev"]]

            def enter(eng):
                def _(e):
                    for t in prev:
                        e.wait_ge(*t.end())
                    if tr[eng]:
                        e.sem_inc(tr[eng].sem, len(tr[eng].steps))
                return _
            for eng in ("scalar", "vector", "gpsimd", "tensor"):
                if tr[eng] or eng != "gpsimd":
                    on(eng)(enter(eng))
            state["prev"] = [t for t in tr.values() if t]
            return tr["scalar"], tr["vector"], tr["tensor"], tr["gpsimd"]

        def use_table(func):
            @on("scalar")
            def _(e):
                e.activation(junk[:, :], ident[:, 0:1], func)

        def c_(i):
            return stat[:, i:i + 4]

        SS, MS, SQ_, RS, TT_ = c_(0), c_(4), c_(8), c_(12), c_(16)

        def rstd_dve(p):
            return [p + n for n in ("ms", "rc", "n1", "n2", "n3", "n4")]

        def emit_rstd(p, a, d, first_wait, scale, eps, src=SS):
            @on("vector")
            def _(e):
                step(e, d, p + "ms", [first_wait], lambda: e.tensor_scalar(MS, src, scale, eps, ALU.mult, ALU.add))
            @on("scalar")
            def _(e):
                step(e, a, p + "sqrt", [d.at(p + "ms")], lambda: e.activation(SQ_, MS, ACT.Sqrt))
            @on("vector")
            def _(e):
                step(e, d, p + "rc", [a.at(p + "sqrt")], lambda: e.reciprocal(RS, SQ_))
                step(e, d, p + "n1", [d.at(p + "rc")], lambda: e.tensor_tensor(TT_, RS, RS, ALU.mult))
                step(e, d, p + "n2", [d.at(p + "n1")], lambda: e.tensor_tensor(TT_, TT_, MS, ALU.mult))
                step(e, d, p + "n3", [d.at(p + "n2")], lambda: e.tensor_scalar(TT_, TT_, -0.5, 1.5, ALU.mult, ALU.add))
                step(e, d, p + "n4", [d.at(p + "n3")], lambda: e.tensor_tensor(RS, RS, TT_, ALU.mult))

        def emit_squares(p, d, src, waits):
            @on("vector")
            def _(e):
                for m in range(MT):
                    step(e, d, f"{p}ss{m}", waits(m) + ([d.at(f"{p}ss{m - 1}")] if m else []), lambda: e.tensor_tensor_reduce(
                        out=tY[:, :, :].rearrange("p a b -> p (a b)"), in0=src[:, m, :], in1=src[:, m, :],
                        scale=1.0, scalar=0.0, op0=ALU.mult, op1=ALU.add, accum_out=SS[:, m:m + 1]))

        def emit_transpose_split(p, a, d, t, src_of, ready, gain):
            @on("tensor")
            def _(e):
                for m in range(MT):
                    for w in ready(m):
                        e.wait_ge(*w)
                    for k in range(KT):
                        last = e.transpose(bank[k][:, P * m:P * m + P], src_of(m)[:, P * k:P * k + P], ident[:, :])
                    t.done(last, f"{p}t{m}")
            g = (lambda k: gains[:, gain + k:gain + k + 1]) if gain is not None else (lambda k: 1.0)
            @on("scalar")
            def _(e):
                for k in range(KT):
                    step(e, a, f"{p}h{k}", [t.at(f"{p}t{MT - 1}")], lambda: e.activation(
                        hT[0][:, k, :], bank[k], ACT.Copy, scale=g(k)))
            @on("vector")
            def _(e):
                for k in range(KT):
                    step(e, d, f"{p}l{k}", [a.at(f"{p}h{k}")], lambda: e.scalar_tensor_tensor(
                        hT[1][:, k, :], bank[k], g(k), hT[0][:, k, :].bitcast(F32), ALU.mult, ALU.subtract))

        def scaled_rows(m):
            return [tU, tZ][m % 2][:, :, :].rearrange("p a b -> p (a b)")

        def emit_norm_to_hT(p, a, d, t, src, ss_waits, gain):
            emit_squares(p, d, src, ss_waits)
            emit_rstd(p, a, d, d.at(f"{p}ss{MT - 1}"), 1.0 / D, RMS_EPS)
            @on("vector")
            def _(e):
                for m in range(MT):
                    w = [d.at(p + "n4")] + ([t.at(f"{p}t{m - 2}")] if m >= 2 else [])
                    step(e, d, f"{p}xn{m}", w, lambda: e.tensor_scalar(
                        scaled_rows(m), src[:, m, :], RS[:, m:m + 1], None, ALU.mult))
            emit_transpose_split(p, a, d, t, lambda m: scaled_rows(m), lambda m: [d.at(f"{p}xn{m}")], gain)

        def norm_steps(p):
            dve = [f"{p}ss{m}" for m in range(MT)] + rstd_dve(p) + [f"{p}xn{m}" for m in range(MT)] + \
                  [f"{p}l{k}" for k in range(KT)]
            act = [p + "sqrt"] + [f"{p}h{k}" for k in range(KT)]
            pe = [f"{p}t{m}" for m in range(MT)]
            return act, dve, pe

        def load_row(to, vec, e):
            e.dma_start(to[:, 0:vec.shape[-1]], vec.partition_broadcast(P)).then_inc(s_row, 16)

        n_const = [0]

        @on("sync")
        def _(e):
            for m in range(MT):
                e.dma_start(x_res[:, m, :], T["x"][0, P * m:P * m + P, :]).then_inc(s_x[m], 16)

        @on("scalar")
        def _(e):
            def put(to, src):
                e.dma_start(to, src).then_inc(s_const, 16)
                n_const[0] += 16
            put(ident[:, :], T["ident"])
            r = rows[:, 0, :]
            for at, name, n in ((G_NORM, "norm_g", 8), (G_POOLB, "pool_b", 8), (G_POOLS, "pool_scale", 8),
                                (G_CONVW, "conv_w", 24), (G_CONVB, "conv_b", 8), (G_ATTN, "attn_pre_norm_2", 8),
                                (G_FFN, "ffn_pre_norm_2", 8)):
                v = T[name]
                src = (v[0].rearrange("t (k c) -> (t k) c", c=P) if len(v.shape) == 3
                       else v[0].rearrange("(k c) -> k c", c=P))
                put(r[at:at + n, :], src)
            put(rows[0:96, 1, :], T["ffn_conv_w_2"][0].rearrange("t (k c) -> (t k) c", c=P))
            put(rows[96:128, 1, :], T["ffn_conv_b_2"][0].rearrange("(k c) -> k c", c=P))
            put(sgu_w[:, :, :], T["sgu_w"][0].rearrange("g i j -> i g j"))
            for k in range(2):
                put(pool_w[:, k, :, :], T["pool_w"][0][:, P * k:P * k + P, :].rearrange("g p d -> p g d"))
            put(ratio[:, :, :], T["ratio"])
            load_row(rowA, T["sgu_ln_g"][0], e)
            load_row(rowB, T["sgu_ln_b"][0], e)
            load_row(rowC, T["sgu_b"][0].rearrange("g i -> (g i)"), e)

        @on("tensor")
        def _(e):
            e.sem_inc(s_used, 2)

        @on("vector")
        def _(e):
            e.sem_inc(s_lo, 2)

        act, dve, pe = norm_steps("n")
        a, d, t, _ = phase("start", ["gain0", "gain1"] + act,
                           ["wt0", "wt1", "mask", "pad"] + dve, ["vec", "wt"] + pe)

        @on("tensor")
        def _(e):
            e.wait_ge(s_const, n_const[0])
            e.transpose(bank[0][:, 0:G_FCW], rows[0:G_FCW, 0, :], ident[0:G_FCW, 0:G_FCW])
            t.done(e.transpose(bank[0][:, P:2 * P], rows[:, 1, :], ident[:, :]), "vec")
            for g in range(SGU_GROUPS):
                last = e.transpose(bank[1 + g // 4][:, P * (g % 4):P * (g % 4) + P], sgu_w[:, g, :], ident[:, :])
            t.done(last, "wt")
            e.wait_ge(*a.at("gain1"))
            e.wait_ge(*d.at("wt1"))

        @on("scalar")
        def _(e):
            step(e, a, "gain0", [t.at("vec")], lambda: e.activation(gains[:, 0:G_FCW], bank[0][:, 0:G_FCW], ACT.Copy))
            step(e, a, "gain1", [], lambda: e.activation(gains[:, G_FCW:G_END], bank[0][:, P:2 * P], ACT.Copy))
            split_hi(e, 0, 0)

        @on("vector")
        def _(e):
            for q in range(2):
                step(e, d, f"wt{q}", [t.at("wt")], lambda: e.tensor_copy(
                    wT[:, 4 * q:4 * q + 4, :], bank[1 + q].rearrange("p (g i) -> p g i", g=4)))
            step(e, d, "mask", [d.at("wt1")], lambda: e.memset(wT[CHUNK:P, :, 0:CHUNK], 0.0))
            step(e, d, "pad", [], lambda: e.memset(padded[:, :, 0:PAD], 0.0))

        emit_norm_to_hT("n", a, d, t, x_res, lambda m: [(s_x[m], 16)], G_NORM)

        @on("vector")
        def _(e):
            split_lo(e, 0, 0)

        H = [0]

        h0 = H[0]
        a, d, t, _ = phase("val", [f"m{m}" for m in range(MT)], [], [f"m{m}" for m in range(MT - 1)], rounds=2)
        use_table(ACT.Gelu_apprx_tanh)

        @on("sync")
        def _(e):
            with e.Fori(0, 2) as c:
                for half in range(2):
                    load(e, h0 + c, half, n_pieces(half, T["w_in"][0], 4 * half, A_V + 512 * c))

        @on("tensor")
        def _(e):
            with e.Fori(0, 2) as c:
                gemm_n(e, h0 + c, hT, [0, 1, 2, 3], lambda m: a.before(f"m{m}", c), t)

        @on("scalar")
        def _(e):
            with e.Fori(0, 2) as c:
                split_hi(e, h0 + c, 1)
                split_hi(e, h0 + c + 1, 0)
                for m in range(MT):
                    step(e, a, f"m{m}", [n_ready(m, t, c, h0 + c)], lambda: e.activation(
                        v_tok[:, m, ds(512 * c, 512)], bank[m], ACT.Gelu_apprx_tanh))

        @on("vector")
        def _(e):
            with e.Fori(0, 2) as c:
                split_lo(e, h0 + c, 1)
                split_lo(e, h0 + c + 1, 0)
        H[0] += 2

        ln = []
        for m in range(MT):
            ln += [f"b{m}0", f"b{m}1", f"ag{m}"]
        a, d, t, _ = phase("ln", ["sqrt"], ln + rstd_dve("") + [f"{o}{m}" for m in range(MT) for o in ("no", "ga", "be")] +
                           [f"mix{g}" for g in range(SGU_GROUPS)], [f"g{g}" for g in range(SGU_GROUPS)])
        bn = stat[:, 20:32].rearrange("p (c s) -> p c s", s=6)
        mv = stat[:, 32:40].rearrange("p (m s) -> p m s", s=2)

        @on("vector")
        def _(e):
            for m in range(MT):
                for c in range(2):
                    w = [d.at(f"ag{m - 1}")] if m else []
                    step(e, d, f"b{m}{c}", w, lambda: e.bn_stats(bn[:, c, :], v_tok[:, m, 512 * c:512 * c + 512]))
                step(e, d, f"ag{m}", [d.at(f"b{m}1")], lambda: e.bn_aggr(mv[:, m, :], stat[:, 20:32]))
        emit_rstd("", a, d, d.at(f"ag{MT - 1}"), 1.0, LN_EPS, src=mv[:, :, 1])

        @on("vector")
        def _(e):
            e.wait_ge(s_row, 48)
            for m in range(MT):
                v = v_tok[:, m, :]
                step(e, d, f"no{m}", [d.at("n4")], lambda: e.tensor_scalar(
                    v, v, mv[:, m, 0:1], RS[:, m:m + 1], ALU.subtract, ALU.mult))
                step(e, d, f"ga{m}", [d.at(f"no{m}")], lambda: e.tensor_tensor(v, v, rowA[:, :], ALU.mult))
                step(e, d, f"be{m}", [d.at(f"ga{m}")], lambda: e.tensor_tensor(v, v, rowB[:, :], ALU.add))

        @on("tensor")
        def _(e):
            e.wait_ge(*d.at(f"be{MT - 1}"))
            for g in range(SGU_GROUPS):
                for m in range(MT):
                    last = e.matmul(bank[g][:, P * m:P * m + P], v_tok[:, m, P * g:P * g + P], wT[:, g, :],
                                    start=True, stop=True)
                t.done(last, f"g{g}")

        @on("vector")
        def _(e):
            for g in range(SGU_GROUPS):
                step(e, d, f"mix{g}", [t.at(f"g{g}")], lambda: e.tensor_tensor(
                    v_tok[:, :, P * g:P * g + P], bank[g].rearrange("p (m i) -> p m i", m=MT),
                    rowC[:, P * g:P * g + P].unsqueeze(1).to_broadcast([P, MT, P]), ALU.add))

        h0 = H[0]
        a, d, t, _ = phase("sgu", ["u", "z", "h"], ["b", "a", "c", "l"], rounds=4)
        use_table(ACT.Gelu_apprx_tanh)

        @on("sync")
        def _(e):
            with e.Fori(0, 4) as j:
                load(e, h0 + j, 0, t_pieces(0, T["w_in"][0], A_U + 256 * j))
                load(e, h0 + j, 1, t_pieces(1, T["w_in"][0], A_Z + 256 * j))

        @on("tensor")
        def _(e, a=a, d=d, h0=h0):
            with e.Fori(0, 4) as j:
                gemm_t(e, h0 + j, 0, hT, (0, 1), [a.before("u", j)])
                gemm_t(e, h0 + j, 1, hT, (2, 3), [d.before("a", j)])

        @on("scalar")
        def _(e, a=a, d=d, h0=h0):
            with e.Fori(0, 4) as j:
                split_hi(e, h0 + j, 1)
                step(e, a, "u", [used(h0 + j, 0), d.before("b", j)],
                     lambda: e.activation(tU[:, :, :], pair[0], ACT.Gelu_apprx_tanh))
                split_hi(e, h0 + j + 1, 0)
                step(e, a, "z", [used(h0 + j, 1), d.before("c", j)],
                     lambda: e.activation(tZ[:, :, :], pair[1], ACT.Tanh, scale=0.5))
                step(e, a, "h", [d.at("c", j)],
                     lambda: e.activation(yT[0][:, ds(2 * j, 2), :], tY[:, :, :], ACT.Copy))

        @on("vector")
        def _(e, a=a, d=d, h0=h0):
            with e.Fori(0, 4) as j:
                split_lo(e, h0 + j, 1)
                e.wait_ge(*a.at("u", j))
                for g in range(2):
                    ins = e.tensor_tensor(tU[:, g, :].rearrange("p (m i) -> p m i", i=P),
                                          tU[:, g, :].rearrange("p (m i) -> p m i", i=P),
                                          v_tok[:, :, ds(2 * P * j + P * g, P)], ALU.mult)
                d.done(ins, "b")
                split_lo(e, h0 + j + 1, 0)
                step(e, d, "a", [a.at("z", j)], lambda: e.scalar_tensor_tensor(
                    tZ[:, :, :], tZ[:, :, :], 1.0, pair[1], ALU.add, ALU.mult))
                step(e, d, "c", [d.at("a", j), a.before("h", j), d.before("l", j)], lambda: e.scalar_tensor_tensor(
                    tY[:, :, :], tZ[:, :, :], 0.5, tU[:, :, :], ALU.mult, ALU.mult))
                step(e, d, "l", [a.at("h", j)], lambda: e.tensor_tensor(
                    yT[1][:, ds(2 * j, 2), :], tY[:, :, :], yT[0][:, ds(2 * j, 2), :].bitcast(F32), ALU.subtract))
        H[0] += 4

        def branch_phase(name, gate_col, w_branch, first):
            h0 = H[0]
            a, d, t, _ = phase(name, ["t"], ["m"] if first else ["m", "s"], rounds=4)
            use_table(ACT.Tanh)

            @on("sync")
            def _(e):
                with e.Fori(0, 4) as j:
                    load(e, h0 + j, 0, t_pieces(0, T["w_in"][0], gate_col + 256 * j))
                    load(e, h0 + j, 1, t_pieces(1, w_branch, 256 * j))

            @on("tensor")
            def _(e):
                with e.Fori(0, 4) as j:
                    gemm_t(e, h0 + j, 0, hT, (0, 1), [a.before("t", j)])
                    gemm_t(e, h0 + j, 1, yT, (2, 3), [d.before("m", j)])

            @on("scalar")
            def _(e):
                with e.Fori(0, 4) as j:
                    split_hi(e, h0 + j, 1)
                    step(e, a, "t", [used(h0 + j, 0), d.before("m", j)],
                         lambda: e.activation(tZ[:, :, :], pair[0], ACT.Tanh, scale=0.5))
                    split_hi(e, h0 + j + 1, 0)

            @on("vector")
            def _(e):
                with e.Fori(0, 4) as j:
                    split_lo(e, h0 + j, 1)
                    split_lo(e, h0 + j + 1, 0)
                    acc = merged[:, ds(2 * j, 2), :]
                    to = acc if first else tY[:, :, :]
                    step(e, d, "m", [a.at("t", j), used(h0 + j, 1)] + ([] if first else [d.before("s", j)]),
                         lambda: e.scalar_tensor_tensor(to, tZ[:, :, :], 1.0, pair[1], ALU.add, ALU.mult))
                    if not first:
                        step(e, d, "s", [d.at("m", j)], lambda: e.tensor_tensor(acc, acc, tY[:, :, :], ALU.add))
            H[0] += 4

        branch_phase("ga", GATES, T["w_branch_a"][0], True)

        h0 = H[0]
        steps_d = []
        for j in range(4):
            steps_d += [f"w{j}{i}" for i in range(j + 1)] + [f"f{j}", f"d{j}", f"a{j}", f"q{j}0", f"q{j}1", f"c{j}", f"l{j}"]
        a, d, t, _ = phase("pool", [f"{o}{j}" for j in range(4) for o in ("p", "z", "h")], steps_d,
                           [f"y{j}" for j in range(4)])
        use_table(ACT.Tanh)

        @on("sync")
        def _(e, h0=h0):
            with e.Fori(0, 4) as j:
                load(e, h0 + j, 0, t_pieces(0, T["w_in"][0], B_P + 256 * j))
                load(e, h0 + j, 1, t_pieces(1, T["w_in"][0], B_Z + 256 * j))

        @on("tensor")
        def _(e, a=a, d=d, t=t, h0=h0):
            for j in range(4):
                gemm_t(e, h0 + j, 0, hT, (0, 1), [a.at(f"p{j - 1}")] if j else [])
                gemm_t(e, h0 + j, 1, hT, (2, 3), [d.at(f"a{j - 1}")] if j else [])
                e.wait_ge(*d.at(f"d{j}"))
                if j:
                    e.wait_ge(*d.at(f"q{j - 1}1"))
                for c in range(2):
                    for k in range(2):
                        last = e.matmul(bank[4 + c], pool_w[:, k, j, P * c:P * c + P], dT[:, k, :],
                                        start=k == 0, stop=k == 1)
                t.done(last, f"y{j}")

        @on("scalar")
        def _(e, a=a, d=d, t=t, h0=h0):
            for j in range(4):
                split_hi(e, h0 + j, 1)
                step(e, a, f"p{j}", [used(h0 + j, 0)] + ([d.at(f"d{j - 1}")] if j else []),
                     lambda: e.activation(padded[:, :, PAD:], pair[0], ACT.Copy))
                split_hi(e, h0 + j + 1, 0)
                step(e, a, f"z{j}", [used(h0 + j, 1)] + ([d.at(f"c{j - 1}")] if j else []),
                     lambda: e.activation(tZ[:, :, :], pair[1], ACT.Tanh, scale=0.5))
                step(e, a, f"h{j}", [d.at(f"c{j}")],
                     lambda: e.activation(yT[0][:, 2 * j:2 * j + 2, :], tY[:, :, :], ACT.Copy))

        @on("vector")
        def _(e, a=a, d=d, t=t, h0=h0):
            for j, win in enumerate(POOL_WINDOWS):
                split_lo(e, h0 + j, 1)
                src, last = padded, [a.at(f"p{j}")]
                for i in range(j + 1):
                    back, lo = 1 << i, (2 << i) - 1
                    dst = (winA, winB)[i % 2]
                    step(e, d, f"w{j}{i}", last, lambda: e.tensor_tensor(
                        dst[:, :, lo:], src[:, :, lo:], src[:, :, lo - back:PAD + S - back], ALU.add))
                    src, last = dst, [d.at(f"w{j}{i}")]
                step(e, d, f"f{j}", last, lambda: e.tensor_tensor(
                    src[:, :, PAD:PAD + win], src[:, :, PAD:PAD + win],
                    ratio[:, j:j + 1, 0:win].to_broadcast([P, 2, win]), ALU.mult))
                step(e, d, f"d{j}", [d.at(f"f{j}")] + ([t.at(f"y{j - 1}")] if j else []), lambda: e.scalar_tensor_tensor(
                    dT[:, :, :], src[:, :, PAD:], 1.0 / win, padded[:, :, PAD:], ALU.mult, ALU.subtract))
                split_lo(e, h0 + j + 1, 0)
                step(e, d, f"a{j}", [a.at(f"z{j}")], lambda: e.scalar_tensor_tensor(
                    tZ[:, :, :], tZ[:, :, :], 1.0, pair[1], ALU.add, ALU.mult))
                for c in range(2):
                    step(e, d, f"q{j}{c}", [t.at(f"y{j}")] + ([d.at(f"l{j - 1}")] if j else []), lambda: e.tensor_scalar(
                        tY[:, c, :], bank[4 + c], gains[:, G_POOLB + 2 * j + c:G_POOLB + 2 * j + c + 1],
                        gains[:, G_POOLS + 2 * j + c:G_POOLS + 2 * j + c + 1], ALU.add, ALU.mult))
                step(e, d, f"c{j}", [d.at(f"q{j}1")], lambda: e.scalar_tensor_tensor(
                    tY[:, :, :], tZ[:, :, :], 0.5, tY[:, :, :], ALU.mult, ALU.mult))
                step(e, d, f"l{j}", [a.at(f"h{j}")], lambda: e.tensor_tensor(
                    yT[1][:, 2 * j:2 * j + 2, :], tY[:, :, :], yT[0][:, 2 * j:2 * j + 2, :].bitcast(F32), ALU.subtract))
        H[0] += 4

        branch_phase("gb", GATES + D, T["w_branch_b"][0], False)

        h0 = H[0]
        a, d, t, _ = phase("conv", ["u", "z", "h"],
                           ["hc", "c00", "c10", "c01", "c11", "c02", "c12", "cb", "a", "c", "l"], rounds=4)
        use_table(ACT.Tanh)

        @on("sync")
        def _(e, h0=h0):
            with e.Fori(0, 4) as j:
                for s_, col in enumerate((C_H, C_C, C_B, C_Z)):
                    load(e, h0 + 2 * j + s_ // 2, s_ % 2, t_pieces(s_ % 2, T["w_in"][0], col + 256 * j))

        @on("tensor")
        def _(e, a=a, d=d, h0=h0):
            with e.Fori(0, 4) as j:
                for s_, free in enumerate((a.before("u", j), d.before("hc", j), d.before("cb", j), d.before("a", j))):
                    gemm_t(e, h0 + 2 * j + s_ // 2, s_ % 2, hT, (2 * s_, 2 * s_ + 1), [free])

        @on("scalar")
        def _(e, a=a, d=d, h0=h0):
            with e.Fori(0, 4) as j:
                hh = h0 + 2 * j
                split_hi(e, hh, 1)
                step(e, a, "u", [used(hh, 0), d.before("hc", j)], lambda: e.activation(tU[:, :, :], pair[0], ACT.Copy))
                split_hi(e, hh + 1, 0)
                split_hi(e, hh + 1, 1)
                split_hi(e, hh + 2, 0)
                step(e, a, "z", [used(hh + 1, 1), d.before("c", j)],
                     lambda: e.activation(tZ[:, :, :], pair[3], ACT.Tanh, scale=0.5))
                step(e, a, "h", [d.at("c", j)],
                     lambda: e.activation(yT[0][:, ds(2 * j, 2), :], tY[:, :, :], ACT.Copy))

        def conv_tap(e, d, j, k, c, tile, w_col, b_col, free):
            src = padded[:, c, PAD - 2 + k:PAD - 2 + k + S]
            w = gains[:, ds(w_col + tile, 1)]
            if k == 0:
                step(e, d, f"c{c}0", free, lambda: e.tensor_scalar(
                    tY[:, c, :], src, w, gains[:, ds(b_col + tile, 1)], ALU.mult, ALU.add))
            else:
                step(e, d, f"c{c}{k}", free, lambda: e.scalar_tensor_tensor(
                    tY[:, c, :], src, w, tY[:, c, :], ALU.mult, ALU.add))

        @on("vector")
        def _(e, a=a, d=d, h0=h0):
            with e.Fori(0, 4) as j:
                hh = h0 + 2 * j
                split_lo(e, hh, 1)
                split_lo(e, hh + 1, 0)
                step(e, d, "hc", [a.at("u", j), used(hh, 1), d.before("c12", j)], lambda: e.tensor_tensor(
                    padded[:, :, PAD:], tU[:, :, :], pair[1], ALU.mult))
                for k in range(TAPS):
                    for c in range(2):
                        free = [d.at("hc", j), d.before("l", j)] if k == 0 else [d.at(f"c{c}{k - 1}", j)]
                        conv_tap(e, d, j, k, c, 2 * j + c, G_CONVW + 8 * k, G_CONVB, free)
                    if k == 0:
                        split_lo(e, hh + 1, 1)
                step(e, d, "cb", [d.at("c12", j), used(hh + 1, 0)], lambda: e.tensor_tensor(
                    tY[:, :, :], tY[:, :, :], pair[2], ALU.mult))
                split_lo(e, hh + 2, 0)
                step(e, d, "a", [a.at("z", j)], lambda: e.scalar_tensor_tensor(
                    tZ[:, :, :], tZ[:, :, :], 1.0, pair[3], ALU.add, ALU.mult))
                step(e, d, "c", [d.at("a", j)], lambda: e.scalar_tensor_tensor(
                    tY[:, :, :], tZ[:, :, :], 0.5, tY[:, :, :], ALU.mult, ALU.mult))
                step(e, d, "l", [a.at("h", j)], lambda: e.tensor_tensor(
                    yT[1][:, ds(2 * j, 2), :], tY[:, :, :], yT[0][:, ds(2 * j, 2), :].bitcast(F32), ALU.subtract))
        H[0] += 8

        branch_phase("gc", GATES + 2 * D, T["w_branch_c"][0], False)

        h0 = H[0]
        a, d, t, _ = phase("split_merged", [f"h{k}" for k in range(KT)], [f"l{k}" for k in range(KT)])

        @on("scalar")
        def _(e, a=a):
            for k in range(KT):
                step(e, a, f"h{k}", [], lambda: e.activation(hT[0][:, k, :], merged[:, k, :], ACT.Copy, scale=0.5))

        @on("vector")
        def _(e, a=a, d=d):
            for k in range(KT):
                step(e, d, f"l{k}", [a.at(f"h{k}")], lambda: e.scalar_tensor_tensor(
                    hT[1][:, k, :], merged[:, k, :], 0.5, hT[0][:, k, :].bitcast(F32), ALU.mult, ALU.subtract))

        MS4 = [f"m{m}" for m in range(MT)]

        def n_phase(name, w, consumer, emit, cols=2):
            h0 = H[0]
            tr = {consumer: MS4}
            a, d, t, _ = phase(name, tr.get("scalar", []), tr.get("vector", []), MS4[:MT - 1], rounds=cols)
            reader = a or d

            @on("sync")
            def _(e):
                with e.Fori(0, cols) as c:
                    for half in range(2):
                        load(e, h0 + c, half, n_pieces(half, w, 4 * half, 512 * c))

            @on("tensor")
            def _(e):
                with e.Fori(0, cols) as c:
                    gemm_n(e, h0 + c, hT, [0, 1, 2, 3], lambda m: reader.before(f"m{m}", c), t)

            for eng, split in (("scalar", split_hi), ("vector", split_lo)):
                def _(e, eng=eng, split=split):
                    with e.Fori(0, cols) as c:
                        split(e, h0 + c, 1)
                        split(e, h0 + c + 1, 0)
                        if eng == consumer:
                            for m in range(MT):
                                step(e, reader, f"m{m}", [n_ready(m, t, c, h0 + c)], lambda: emit(e, m, c))
                on(eng)(_)
            H[0] += cols

        @on("scalar")
        def _(e):
            load_row(rowA, T["final_g"], e)

        n_phase("w_out", T["w_out"][0], "vector", lambda e, m, c: e.tensor_tensor(
            x_res[:, m, ds(512 * c, 512)], x_res[:, m, ds(512 * c, 512)], bank[m], ALU.add))

        two = ExitStack()
        qk = sb("qk", [P, 16, S], stack=two)
        att_v = sb("att_v", [P, MT, D], stack=two)
        mix = sb("mix", [P, MT, D], stack=two)
        causal = sb("causal", [P, S], stack=two)
        banded = sb("banded", [P, 2 * P], stack=two)
        cmp_dist = sb("cmp_dist", [P, MT, N_CMP], stack=two)
        cmp_mask = sb("cmp_mask", [P, MT, N_CMP], stack=two)
        cmp_s = sb("cmp_s", [P, 2, MT, N_CMP], stack=two)
        slopes = sb("slopes", [P, 16], stack=two)
        sinks = sb("sinks", [P, HEADS], stack=two)
        lam_in = sb("lam_in", [P, 4, DQ], stack=two)
        subln = sb("subln", [P, DH], stack=two)
        pos_rows = sb("pos_rows", [CMP_LEN, P], stack=two)
        pos = sb("pos", [P, CMP_LEN], stack=two)
        b1 = sb("b1", [P, 2], stack=two)
        w2 = sb("w2", [P, 2, DH], stack=two)
        hid = sb("hid", [P, 2, N_CMP], stack=two)
        kcT = sb("kcT", [DH, N_CMP], stack=two)
        vc = sb("vc", [N_CMP, DH], stack=two)
        gate = sb("gate", [P, MT, 3 * HEADS], stack=two)
        small = sb("small", [P, 128], stack=two)
        two.close()
        scores = tU
        probT = tZ
        bias = tY
        fixed_k = rowA[0:DH, :].rearrange("p (n s) -> p n s", n=2)
        head_k = rowB[0:DH, :].rearrange("p (n s) -> p n s", n=2)
        head_q = rowC[0:DH, :].rearrange("p (n s) -> p n s", n=2)
        w1 = mix[:, :, :].rearrange("p m (l f) -> p (m l) f", f=CMP_HID)
        T_MQ, T_MK, T_NQ, T_CMP, T_SLC, T_WIN, T_SK, T_DQ, T_DK, T_SQ = 0, 2, 4, 6, 7, 8, 9, 10, 12, 14
        V_M, V_D, V_SLC, V_WIN, V_GATE, V_S = 0, 256, 512, 640, 704, 716
        V_WIDTH = (512, V_S - 512 + 128)

        act, dve, pe = norm_steps("b")
        a, d, t, _ = phase("fin", ["fsqrt"] + act, [f"fss{m}" for m in range(MT)] + rstd_dve("f") +
                           [f"x{m}" for m in range(MT)] + dve, pe)
        emit_squares("f", d, x_res, lambda m: [])
        emit_rstd("f", a, d, d.at(f"fss{MT - 1}"), 1.0 / D, RMS_EPS)

        @on("vector")
        def _(e):
            e.wait_ge(s_row, 64)
            for m in range(MT):
                step(e, d, f"x{m}", [d.at("fn4")], lambda: e.scalar_tensor_tensor(
                    x_res[:, m, :], x_res[:, m, :], RS[:, m:m + 1], rowA[:, :], ALU.mult, ALU.mult))
        emit_norm_to_hT("b", a, d, t, x_res, lambda m: [d.at(f"x{m}")], G_ATTN)

        h0 = H[0]
        a, d, t, _ = phase("proj", ["c"], ["c"], rounds=4)
        n_att = [0]

        @on("scalar")
        def _(e):
            def put(to, src):
                e.dma_start(to, src).then_inc(s_att, 16)
                n_att[0] += 16
            put(causal[:, :], T["causal"])
            put(banded[:, :], T["banded"])
            put(cmp_dist[:, :, :], T["cmp_dist"])
            put(cmp_mask[:, :, :], T["cmp_mask"])
            put(slopes[:, :], T["slopes"])
            put(sinks[:, :], T["swa_sinks_2"][0].partition_broadcast(P))
            for n, name in enumerate(("q1", "k1", "q2", "k2")):
                put(lam_in[:, n, :], T[f"diff_lambda_{name}_2"][0].partition_broadcast(P))
            put(subln[:, :], T["diff_subln_2"][0].partition_broadcast(P))
            for n, name in enumerate(("k", "v")):
                rows_ = slice(DH * n, DH * n + DH)
                put(pos_rows[:, rows_], T[f"nsa_cmp_pos_{name}_2"][0])
                put(w1[rows_, :, :], T[f"nsa_cmp_w1_{name}_2"][0].rearrange("l d f -> d l f"))
                put(b1[:, n:n + 1], T[f"nsa_cmp_b1_{name}_2"][0].rearrange("(f o) -> f o", o=1))
                put(w2[:, n, :], T[f"nsa_cmp_w2_{name}_2"][0])

        @on("sync")
        def _(e):
            w = T["w_in_2"][0]
            for n, col in enumerate((MQ, MK, NQ, NKC, None, DQ_, DK_, SQ)):
                slot = n % 2
                if col is None:
                    to = raw[slot][:, :].rearrange("p (k c) -> p k c", k=KT)
                    src = w.rearrange("(k p) c -> p k c", p=P)
                    pieces = [(to[:, :, 0:P], src[:, :, NKW:NKW + P]), (to[:, :, P:2 * P], src[:, :, SK:SK + P])]
                else:
                    pieces = t_pieces(slot, w, col)
                load(e, h0 + n // 2, slot, pieces)

        @on("tensor")
        def _(e):
            with e.Fori(0, 4) as j:
                gemm_t(e, h0 + j, 0, hT, (0, 1), [a.before("c", j)])
                gemm_t(e, h0 + j, 1, hT, (2, 3), [d.before("c", j)])

        @on("scalar")
        def _(e):
            with e.Fori(0, 4) as j:
                split_hi(e, h0 + j, 1)
                step(e, a, "c", [used(h0 + j, 0)], lambda: e.activation(qk[:, ds(4 * j, 2), :], pair[0], ACT.Copy))
                split_hi(e, h0 + j + 1, 0)

        @on("vector")
        def _(e):
            with e.Fori(0, 4) as j:
                split_lo(e, h0 + j, 1)
                split_lo(e, h0 + j + 1, 0)
                step(e, d, "c", [used(h0 + j, 1)], lambda: e.tensor_copy(qk[:, ds(4 * j + 2, 2), :], pair[1]))
        H[0] += 4

        h0 = H[0]
        a, d, t, _ = phase("projv", MS4, [], MS4[:MT - 1], rounds=2)

        @on("sync")
        def _(e):
            w = T["w_in_2"][0].rearrange("(k p) c -> p k c", p=P)
            for c, parts in enumerate((((MV, 256), (DV, 256)), ((NVS, 204), (SV, 128)))):
                for half in range(2):
                    to = raw[half][:, :].rearrange("p (k c) -> p k c", k=4)
                    at, pieces = 0, []
                    for col, n in parts:
                        pieces.append((to[:, :, at:at + n], w[:, 4 * half:4 * half + 4, col:col + n]))
                        at += n
                    load(e, h0 + c, half, pieces)

        @on("tensor")
        def _(e):
            for c in range(2):
                gemm_n(e, h0 + c, hT, [0, 1, 2, 3], lambda m: a.before(f"m{m}", c), t, V_WIDTH[c])

        @on("scalar")
        def _(e):
            for c in range(2):
                split_hi(e, h0 + c, 1)
                split_hi(e, h0 + c + 1, 0)
                for m in range(MT):
                    step(e, a, f"m{m}", [n_ready(m, t, c, h0 + c)], lambda: e.activation(
                        att_v[:, m, 512 * c:512 * c + V_WIDTH[c]], bank[m][:, 0:V_WIDTH[c]], ACT.Copy))

        @on("vector")
        def _(e):
            for c in range(2):
                split_lo(e, h0 + c, 1)
                split_lo(e, h0 + c + 1, 0)
        H[0] += 2

        MX, DEN, ESK, COEF = (small[:, 8 * n:8 * n + 8] for n in range(4))
        LAM, SUM2, EXP2 = small[:, 40:41], small[:, 41:43], small[:, 43:45]
        DSS, DMS, DSQ, DRS, DT = (small[:, 48 + 16 * n:64 + 16 * n] for n in range(5))
        a, d, t, _ = phase("cmp", ["gk", "gv", "gate", "lam"],
                           ["pos", "ka", "kb", "kc", "vc", "gate", "l1", "l2", "l3", "l4", "sub", "k0", "k1"],
                           ["pos", "hk", "hv", "kc", "vc"])
        kA = padded[:, 0, 0:16 * N_CMP].rearrange("p (n l) -> p n l", l=16)
        kB = padded[:, 1, 0:16 * N_CMP].rearrange("p (n l) -> p n l", l=16)

        @on("tensor")
        def _(e):
            e.wait_ge(s_att, n_att[0])
            t.done(e.transpose(bank[0][:, 0:CMP_LEN], pos_rows[:, :], ident[0:CMP_LEN, 0:CMP_LEN]), "pos")
            for n, name in enumerate(("hk", "hv")):
                r = slice(DH * n, DH * n + DH)
                for l in range(CMP_LEN):
                    if l % 16 == 0 and n == 0:
                        e.wait_ge(*d.at("ka" if l == 0 else "kb"))
                    src = kA if l < 16 else kB
                    last = e.matmul(bank[1 + n][:, 0:N_CMP], w1[r, l, :], src[r, :, l % 16],
                                    start=l == 0, stop=l == CMP_LEN - 1)
                t.done(last, name)
            e.wait_ge(*a.at("gk"))
            t.done(e.matmul(bank[3][0:DH, 0:N_CMP], w2[:, 0, :], hid[:, 0, :], start=True, stop=True), "kc")
            e.wait_ge(*a.at("gv"))
            t.done(e.matmul(bank[4][0:N_CMP, 0:DH], hid[:, 1, :], w2[:, 1, :], start=True, stop=True), "vc")

        @on("vector")
        def _(e):
            step(e, d, "pos", [t.at("pos")], lambda: e.tensor_copy(pos[:, :], bank[0][:, 0:CMP_LEN]))
            for n, (name, to) in enumerate((("ka", kA), ("kb", kB))):
                step(e, d, name, [d.at("pos")], lambda: e.tensor_tensor(
                    to, qk[:, T_CMP, 16 * n:16 * n + 16 * N_CMP].rearrange("p (n l) -> p n l", l=16),
                    pos[:, 16 * n:16 * n + 16].unsqueeze(1).to_broadcast([P, N_CMP, 16]), ALU.add))
            step(e, d, "kc", [t.at("kc")], lambda: e.tensor_copy(kcT[:, :], bank[3][0:DH, 0:N_CMP]))
            step(e, d, "vc", [t.at("vc")], lambda: e.tensor_copy(vc[:, :], bank[4][0:N_CMP, 0:DH]))
            step(e, d, "gate", [a.at("gate")], lambda: e.tensor_scalar(
                gate[:, :, :], gate[:, :, :], 0.5, 0.5, ALU.mult, ALU.add))
            for n in range(2):
                step(e, d, f"l{n + 1}", [], lambda: e.tensor_tensor_reduce(
                    out=small[:, 96 - 32 * n:128 - 32 * n],
                    in0=lam_in[:, 2 * n, :], in1=lam_in[:, 2 * n + 1, :], scale=1.0,
                    scalar=0.0, op0=ALU.mult, op1=ALU.add, accum_out=SUM2[:, n:n + 1]))
            step(e, d, "l3", [a.at("lam")], lambda: e.tensor_tensor(LAM, EXP2[:, 0:1], EXP2[:, 1:2], ALU.subtract))
            step(e, d, "l4", [d.at("l3")], lambda: e.tensor_scalar(LAM, LAM, LAMBDA_INIT, None, ALU.add))
            step(e, d, "sub", [], lambda: e.tensor_scalar(subln[:, :], subln[:, :], 1.0 - LAMBDA_INIT, None, ALU.mult))
            step(e, d, "k0", [], lambda: e.tensor_copy(fixed_k[:, 0, :], qk[0:DH, T_SLC, :]))
            step(e, d, "k1", [], lambda: e.tensor_copy(fixed_k[:, 1, :], qk[0:DH, T_WIN, :]))

        @on("scalar")
        def _(e):
            for n, name in enumerate(("gk", "gv")):
                step(e, a, name, [t.at(("hk", "hv")[n])], lambda: e.activation(
                    hid[:, n, :], bank[1 + n][:, 0:N_CMP], ACT.Gelu_apprx_tanh, bias=b1[:, n:n + 1]))
            step(e, a, "gate", [], lambda: e.activation(
                gate[:, :, :], att_v[:, :, V_GATE:V_GATE + 3 * HEADS], ACT.Tanh, scale=0.5))
            step(e, a, "lam", [d.at("l2")], lambda: e.activation(EXP2, SUM2, ACT.Exp))

        dn = ["d", "s", "m", "x", "k", "den", "mn", "r", "g", "p", "o"]
        a, d, t, _ = phase("cmpatt", [f"{o}{b}" for b in range(2) for o in "qe"],
                           [f"{o}{b}" for b in range(2) for o in dn],
                           [f"{o}{b}" for b in range(2) for o in "STV"], rounds=2)
        use_table(ACT.Exp)

        @on("scalar")
        def _(e):
            with e.Fori(0, 2) as i:
                for b in range(2):
                    step(e, a, f"q{b}", [t.before(f"S{b}", i)], lambda: e.activation(
                        head_q[:, b, :], qk[DH * b:DH * b + DH, ds(T_NQ + i, 1), :].rearrange("p o s -> p (o s)"),
                        ACT.Copy, scale=DH ** -0.5))
                    step(e, a, f"e{b}", [d.at(f"x{b}", i)], lambda: e.activation(
                        cmp_s[:, b, :, :], cmp_s[:, b, :, :], ACT.Exp))

        @on("tensor")
        def _(e):
            with e.Fori(0, 2) as i:
                for b in range(2):
                    e.wait_ge(*a.at(f"q{b}", i))
                    e.wait_ge(*d.before(f"s{b}", i))
                    for r in range(MT):
                        last = e.matmul(bank[b][:, 32 * r:32 * r + N_CMP], head_q[:, b, P * r:P * r + P], kcT[:, :],
                                        start=True, stop=True)
                    t.done(last, f"S{b}")
                    e.wait_ge(*d.at(f"k{b}", i))
                    e.wait_ge(*d.before(f"p{b}", i))
                    for r in range(MT):
                        last = e.transpose(bank[2 + b][0:N_CMP, P * r:P * r + P], cmp_s[:, b, r, :], ident[:, :])
                    t.done(last, f"T{b}")
                    e.wait_ge(*d.at(f"p{b}", i))
                    e.wait_ge(*d.before(f"o{b}", i))
                    for r in range(MT):
                        last = e.matmul(bank[4 + b][:, DH * r:DH * r + DH], probT[0:N_CMP, b, P * r:P * r + P], vc[:, :],
                                        start=True, stop=True)
                    t.done(last, f"V{b}")

        def quarter(x, b):
            return x[:, 4 * b:4 * b + 4]

        def over(x, shape):
            return x.unsqueeze(2).to_broadcast(shape)

        def heads_out(b):
            return bank[4 + b][:, 0:MT * DH].rearrange("p (m c) -> p m c", m=MT)

        def gate_of(i, b, g):
            return gate[:, :, ds(6 * i + 3 * b + g, 1)].rearrange("p m o -> p (m o)")

        @on("vector")
        def _(e):
            with e.Fori(0, 2) as i:
                for b in range(2):
                    s_, flat = cmp_s[:, b, :, :], [P, MT, N_CMP]
                    at = lambda n: d.at(f"{n}{b}", i)
                    step(e, d, f"d{b}", [t.before(f"T{b}", i)], lambda: e.tensor_scalar(
                        s_, cmp_dist[:, :, :], slopes[:, ds(4 + 2 * i + b, 1)], None, ALU.mult))
                    step(e, d, f"s{b}", [at("d"), t.at(f"S{b}", i)], lambda: e.tensor_tensor(
                        s_, s_, bank[b][:, 0:128].rearrange("p (m n) -> p m n", m=MT)[:, :, 0:N_CMP], ALU.add))
                    step(e, d, f"m{b}", [at("s")], lambda: e.tensor_reduce(quarter(MX, b), s_, AX.X, ALU.max))
                    step(e, d, f"x{b}", [at("m")], lambda: e.tensor_tensor(s_, s_, over(quarter(MX, b), flat), ALU.subtract))
                    step(e, d, f"k{b}", [a.at(f"e{b}", i)], lambda: e.tensor_tensor(s_, s_, cmp_mask[:, :, :], ALU.mult))
                    step(e, d, f"den{b}", [at("k")], lambda: e.tensor_reduce(quarter(DEN, b), s_, AX.X, ALU.add))
                    step(e, d, f"mn{b}", [at("den")], lambda: e.tensor_scalar(quarter(DEN, b), quarter(DEN, b), TINY, None, ALU.max))
                    step(e, d, f"r{b}", [at("mn")], lambda: e.reciprocal(quarter(COEF, b), quarter(DEN, b)))
                    step(e, d, f"g{b}", [at("r")], lambda: e.tensor_tensor(
                        quarter(COEF, b), quarter(COEF, b), gate_of(i, b, 0), ALU.mult))
                    step(e, d, f"p{b}", [t.at(f"T{b}", i), t.before(f"V{b}", i)], lambda: e.tensor_copy(
                        probT[0:N_CMP, b, :], bank[2 + b][0:N_CMP, :]))
                    step(e, d, f"o{b}", [t.at(f"V{b}", i), at("g")], lambda: e.tensor_tensor(
                        mix[:, :, ds(256 + 2 * DH * i + DH * b, DH)], heads_out(b), over(quarter(COEF, b), [P, MT, DH]), ALU.mult))

        def attention(name, jobs, rounds, q_tile, k_tile, k_fixed, v_col, slope, dk, table, finish, finish_steps,
                      release, scale, sink=None):
            W = table.shape[-1]
            span = lambda r: (max(0, r - 1) if W < S else 0, r + 1)
            units = [(b, r) for b in range(jobs) for r in range(MT)]
            U = len(units)
            nm = lambda o, u: f"{o}{units[u][0]}{units[u][1]}"
            act, dve, pe, pool = [], [], [], [f"s{b}" for b in range(jobs)]
            act += ["q0", "q1"]
            for u in range(U):
                act.append(nm("e", u))
                b, r = units[u]
                if r == MT - 1:
                    if sink is not None:
                        act.append(f"x{b}")
                    if b + 2 < jobs:
                        act.append(f"q{b + 2}")
            staged = k_fixed is None
            if staged:
                dve += ["k0", "k1"]
            order = []
            for u in range(U + 1):
                if u < U:
                    order += [("t", u), ("n", u)]
                if u >= 1:
                    order.append(("p", u - 1))
                    b, r = units[u - 1]
                    if r == 0 and b >= 1:
                        order.append(("f", b - 1))
                        if staged and b + 1 < jobs:
                            order.append(("k", b + 1))
            order.append(("f", jobs - 1))
            for o, u in order:
                dve += finish_steps(u) if o == "f" else [f"k{u}"] if o == "k" else [nm(o, u)]
            pe_order = [("S", 0), ("S", 1)]
            for u in range(U):
                pe_order.append(("T", u))
                if u + 2 < U:
                    pe_order.append(("S", u + 2))
                if u >= 1:
                    pe_order.append(("V", u - 1))
            pe_order.append(("V", U - 1))
            pe = [nm(o, u) for o, u in pe_order]
            a, d, t, g = phase(name, act, dve, pe, pool, rounds=rounds)
            use_table(ACT.Exp)

            def back(track, o, u, i):
                return track.at(nm(o, u), i) if u >= 0 else track.before(nm(o, u + U), i)

            def back_job(track, label, b, i):
                return track.at(label(b), i) if b >= 0 else track.before(label(b + jobs), i)

            rows = lambda b: q_rows(b, dk)

            @on("gpsimd")
            def _(e):
                with e.Fori(0, rounds) as i:
                    for b in range(jobs):
                        step(e, g, f"s{b}", [back_job(d, lambda x: f"t{x}{MT - 1}", b - 2, i)], lambda: e.tensor_tensor(
                            bias[:, b % 2, 0:W], table[:, :], slopes[:, ds(slope(i, b), 1)].to_broadcast([P, W]), ALU.mult), s_gate)

            @on("scalar")
            def _(e):
                def query(b, i):
                    step(e, a, f"q{b}", [back_job(t, lambda x: f"S{x}{MT - 1}", b - 2, i)], lambda: e.activation(
                        head_q[0:dk, b % 2, :], qk[rows(b), ds(q_tile(i), 1), :].rearrange("p o s -> p (o s)"),
                        ACT.Copy, scale=scale))
                with e.Fori(0, rounds) as i:
                    query(0, i)
                    query(1, i)
                    for u in range(U):
                        b, r = units[u]
                        lo, hi = span(r)
                        w, col = P * (hi - lo), 4 * (b % 2) + r
                        step(e, a, nm("e", u), [d.at(nm("n", u), i)], lambda: e.activation(
                            scores[:, u % 2, 0:w], scores[:, u % 2, 0:w], ACT.Exp, bias=MX[:, col:col + 1],
                            accum_out=DEN[:, col:col + 1]))
                        if r == MT - 1:
                            if sink is not None:
                                step(e, a, f"x{b}", [], lambda: e.activation(
                                    quarter(ESK, b % 2), quarter(MX, b % 2), ACT.Exp, bias=sink(i, b)))
                            if b + 2 < jobs:
                                query(b + 2, i)

            @on("tensor")
            def _(e):
                with e.Fori(0, rounds) as i:
                    for o, u in pe_order:
                        b, r = units[u]
                        lo, hi = span(r)
                        w = P * (hi - lo)
                        if o == "S":
                            if r == 0:
                                e.wait_ge(*a.at(f"q{b}", i))
                            if u == 0 and staged:
                                e.wait_ge(*d.at("k0", i))
                            else:
                                e.wait_ge(*back(d, "t", u - 2, i))
                            stand(e, s_gate)
                            keys = head_k[0:dk, b % 2, P * lo:P * hi] if staged else k_fixed(i, P * lo, P * hi)
                            last = e.matmul(bank[u % 2][:, 0:w], head_q[0:dk, b % 2, P * r:P * r + P], keys,
                                            start=True, stop=True)
                        elif o == "T":
                            e.wait_ge(*a.at(nm("e", u), i))
                            e.wait_ge(*back(d, "p", u - 2, i))
                            for n in range(hi - lo):
                                last = e.transpose(bank[2 + u % 2][:, P * n:P * n + P],
                                                   scores[:, u % 2, P * n:P * n + P], ident[:, :])
                        else:
                            need = [nm("p", u)] + ([release(b - 2)] if r == 0 and b >= 2 else [])
                            e.wait_ge(*d.at(max(need, key=d.steps.index), i))
                            stand(e, s_gate)
                            for n in range(hi - lo):
                                last = e.matmul(bank[4 + b % 2][:, DH * r:DH * r + DH], probT[:, u % 2, P * n:P * n + P],
                                                att_v[:, lo + n, ds(v_col(i, b), DH)], start=n == 0, stop=n == hi - lo - 1)
                        t.done(last, nm(o, u))

            @on("vector")
            def _(e):
                def key(b, i):
                    step(e, d, f"k{b}", [back_job(t, lambda x: f"S{x}{MT - 1}", b - 2, i)], lambda: e.tensor_copy(
                        head_k[0:dk, b % 2, :], qk[rows(b), ds(k_tile(i), 1), :].rearrange("p o s -> p (o s)")))
                with e.Fori(0, rounds) as i:
                    if staged:
                        key(0, i)
                        key(1, i)
                    for o, u in order:
                        if o == "f":
                            finish(e, d, t, i, u, a)
                            continue
                        if o == "k":
                            key(u, i)
                            continue
                        b, r = units[u]
                        lo, hi = span(r)
                        w, col = P * (hi - lo), 4 * (b % 2) + r
                        if o == "t":
                            at = W - P + P * (lo - r)
                            step(e, d, nm("t", u), [t.at(nm("S", u), i), g.at(f"s{b}", i)],
                                 lambda: e.tensor_tensor_reduce(
                                     out=scores[:, u % 2, 0:w], in0=bank[u % 2][:, 0:w], in1=bias[:, b % 2, at:at + w],
                                     scale=1.0, scalar=-3e38, op0=ALU.add, op1=ALU.max, accum_out=MX[:, col:col + 1]), s_gate)
                        elif o == "n":
                            m = MX[:, col:col + 1]
                            if sink is None:
                                step(e, d, nm("n", u), [d.at(nm("t", u), i)], lambda: e.tensor_scalar(m, m, -1.0, None, ALU.mult))
                            else:
                                step(e, d, nm("n", u), [d.at(nm("t", u), i)], lambda: e.tensor_scalar(
                                    m, m, sink(i, b), -1.0, ALU.max, ALU.mult))
                        else:
                            step(e, d, nm("p", u), [t.at(nm("T", u), i), back(t, "V", u - 2, i)], lambda: e.tensor_copy(
                                probT[:, u % 2, 0:w], bank[2 + u % 2][:, 0:w]))

        def q_rows(b, dk):
            return slice(dk * b, dk * b + dk)

        def gated(branch):
            def finish(e, d, t, i, b, a):
                c = quarter(COEF, b % 2)
                step(e, d, f"r{b}", [t.at(f"V{b}3", i)], lambda: e.reciprocal(c, quarter(DEN, b % 2)))
                step(e, d, f"g{b}", [d.at(f"r{b}", i)], lambda: e.tensor_tensor(c, c, gate_of(i, b, branch), ALU.mult))
                part = padded[:, 0, 0:MT * DH].rearrange("p (m c) -> p m c", m=MT)
                to = mix[:, :, ds(256 + 2 * DH * i + DH * b, DH)]
                step(e, d, f"w{b}", [d.at(f"g{b}", i)], lambda: e.tensor_tensor(
                    part, heads_out(b % 2), over(c, [P, MT, DH]), ALU.mult))
                step(e, d, f"o{b}", [d.at(f"w{b}", i)], lambda: e.tensor_tensor(to, to, part, ALU.add))
            return finish, lambda b: [f"{o}{b}" for o in "rgwo"], lambda b: f"w{b}"

        for branch, (label, k_at, v_at) in enumerate((("slc", 0, V_SLC), ("win", 1, V_WIN))):
            finish, names, release = gated(1 + branch)
            attention(label, 2, 2, lambda i: T_NQ + i, None, lambda i, lo, hi: fixed_k[:, k_at, lo:hi],
                      lambda i, b: v_at, lambda i, b: 4 + 2 * i + b, DH, causal, finish, names, release, DH ** -0.5)

        def plain(col, with_sink):
            def finish(e, d, t, i, b, a):
                c = quarter(COEF, b % 2)
                w = [t.at(f"V{b}3", i)]
                if with_sink:
                    step(e, d, f"y{b}", [a.at(f"x{b}", i)], lambda: e.tensor_tensor(
                        quarter(DEN, b % 2), quarter(DEN, b % 2), quarter(ESK, b % 2), ALU.add))
                    w.append(d.at(f"y{b}", i))
                step(e, d, f"r{b}", w, lambda: e.reciprocal(c, quarter(DEN, b % 2)))
                step(e, d, f"o{b}", [d.at(f"r{b}", i)], lambda: e.tensor_tensor(
                    mix[:, :, ds(col + 2 * DH * i + DH * b, DH)], heads_out(b % 2), over(c, [P, MT, DH]), ALU.mult))
            return finish, lambda b: [f"{o}{b}" for o in ("yro" if with_sink else "ro")], lambda b: f"o{b}"

        finish, names, release = plain(0, False)
        attention("moba", 2, 2, lambda i: T_MQ + i, lambda i: T_MK + i, None,
                  lambda i, b: V_M + 2 * DH * i + DH * b, lambda i, b: 2 * i + b, DH, causal, finish, names, release, DH ** -0.5)

        def diff_finish(e, d, t, i, b, a):
            c = [quarter(COEF, n) for n in range(2)]
            step(e, d, f"r{b}", [t.at(f"V{b}3", i)], lambda: e.reciprocal(c[b % 2], quarter(DEN, b % 2)))
            if b % 2 == 0:
                return
            part = padded[:, 0, 0:MT * DH].rearrange("p (m c) -> p m c", m=MT)
            to = mix[:, :, ds(512 + 2 * DH * i + DH * (b // 2), DH)]
            step(e, d, f"g{b}", [d.at(f"r{b}", i)], lambda: e.tensor_scalar(c[1], c[1], LAM, None, ALU.mult))
            step(e, d, f"w{b}", [d.at(f"g{b}", i)], lambda: e.tensor_tensor(
                part, heads_out(1), over(c[1], [P, MT, DH]), ALU.mult))
            step(e, d, f"v{b}", [d.at(f"r{b}", i)], lambda: e.tensor_tensor(
                to, heads_out(0), over(c[0], [P, MT, DH]), ALU.mult))
            step(e, d, f"o{b}", [d.at(f"w{b}", i), d.at(f"v{b}", i)], lambda: e.tensor_tensor(to, to, part, ALU.subtract))

        attention("diff", 4, 2, lambda i: T_DQ + i, lambda i: T_DK + i, None,
                  lambda i, b: V_D + 2 * DH * i + DH * (b // 2), lambda i, b: 8 + 2 * i + b // 2, DQ, causal,
                  diff_finish, lambda b: [f"{o}{b}" for o in ("rgwvo" if b % 2 else "r")], lambda b: f"v{b | 1}", DQ ** -0.5)

        a, d, t, _ = phase("dnorm", ["sqrt"], ["sq", "ss", "ms", "rc", "n1", "n2", "n3", "n4", "o", "g", "k0", "k1"])
        o4 = mix[:, :, 512:768].rearrange("p m (h c) -> p m h c", c=DH)
        sq4 = tY[:, :, :].rearrange("p a (b h c) -> p (a b) h c", c=DH, h=4)
        m4 = lambda x: x.rearrange("p (m h) -> p m h", h=4)

        @on("vector")
        def _(e):
            step(e, d, "sq", [], lambda: e.tensor_tensor(sq4, o4, o4, ALU.mult))
            step(e, d, "ss", [d.at("sq")], lambda: e.tensor_reduce(
                DSS, tY[:, :, :].rearrange("p a (b c) -> p (a b) c", c=DH), AX.X, ALU.add))
            step(e, d, "ms", [d.at("ss")], lambda: e.tensor_scalar(DMS, DSS, 1.0 / DH, RMS_EPS, ALU.mult, ALU.add))
            step(e, d, "rc", [a.at("sqrt")], lambda: e.reciprocal(DRS, DSQ))
            step(e, d, "n1", [d.at("rc")], lambda: e.tensor_tensor(DT, DRS, DRS, ALU.mult))
            step(e, d, "n2", [d.at("n1")], lambda: e.tensor_tensor(DT, DT, DMS, ALU.mult))
            step(e, d, "n3", [d.at("n2")], lambda: e.tensor_scalar(DT, DT, -0.5, 1.5, ALU.mult, ALU.add))
            step(e, d, "n4", [d.at("n3")], lambda: e.tensor_tensor(DRS, DRS, DT, ALU.mult))
            step(e, d, "o", [d.at("n4")], lambda: e.tensor_tensor(
                o4, o4, m4(DRS).unsqueeze(3).to_broadcast([P, MT, 4, DH]), ALU.mult))
            step(e, d, "g", [d.at("o")], lambda: e.tensor_tensor(
                o4, o4, subln[:, :].unsqueeze(1).unsqueeze(1).to_broadcast([P, MT, 4, DH]), ALU.mult))
            for n in range(2):
                step(e, d, f"k{n}", [], lambda: e.tensor_copy(fixed_k[:, n, :], qk[DH * n:DH * n + DH, T_SK, :]))

        @on("scalar")
        def _(e):
            step(e, a, "sqrt", [d.at("ms")], lambda: e.activation(DSQ, DMS, ACT.Sqrt))

        finish, names, release = plain(768, True)
        attention("swa", 2, 2, lambda i: T_SQ + i, None,
                  lambda i, lo, hi: fixed_k[:, ds(i, 1), lo:hi].rearrange("p o s -> p (o s)"),
                  lambda i, b: V_S + DH * i, lambda i, b: 12 + 2 * i + b, DH, banded, finish, names, release, DH ** -0.5,
                  sink=lambda i, b: sinks[:, ds(2 * i + b, 1)])

        a, d, t, _ = phase("mixT", [f"xh{k}" for k in range(KT)], [f"xl{k}" for k in range(KT)],
                           [f"xt{m}" for m in range(MT)])
        emit_transpose_split("x", a, d, t, lambda m: mix[:, m, :], lambda m: [], None)

        @on("scalar")
        def _(e):
            load_row(rowA, T["attn_post_norm_2"][0], e)
            load_row(rowB, T["ffn_post_norm_2"][0], e)

        n_phase("w_out2", T["w_out_2"][0], "scalar", lambda e, m, c: e.activation(
            att_v[:, m, ds(512 * c, 512)], bank[m], ACT.Copy))

        act, dve, pe = norm_steps("g")
        a, d, t, _ = phase("post", ["psqrt"] + act, [f"pss{m}" for m in range(MT)] + rstd_dve("p") +
                           [f"{o}{m}" for m in range(MT) for o in "wx"] + dve, pe)
        emit_squares("p", d, att_v, lambda m: [])
        emit_rstd("p", a, d, d.at(f"pss{MT - 1}"), 1.0 / D, RMS_EPS)

        @on("vector")
        def _(e):
            e.wait_ge(s_row, 96)
            for m in range(MT):
                step(e, d, f"w{m}", [d.at("pn4")], lambda: e.scalar_tensor_tensor(
                    att_v[:, m, :], att_v[:, m, :], RS[:, m:m + 1], rowA[:, :], ALU.mult, ALU.mult))
                step(e, d, f"x{m}", [d.at(f"w{m}")], lambda: e.tensor_tensor(
                    x_res[:, m, :], x_res[:, m, :], att_v[:, m, :], ALU.add))
        emit_norm_to_hT("g", a, d, t, x_res, lambda m: [d.at(f"x{m}")], G_FFN)

        three = ExitStack()
        ff = [sb("ff_hi", [P, KT, S], F32R, three), sb("ff_lo", [P, KT, S], F32R, three)]
        acc = sb("acc", [P, MT, D], stack=three)
        three.close()
        h0 = H[0]
        a, d, t, g = phase("up", ["g", "e", "h"], ["c00", "c10", "c01", "c11", "c02", "c12", "m", "l"], rounds=4 * FCH)
        a2 = Track(sem("down_vector"), MS4, 2 * FCH)
        t2 = Track(sem("down_tensor"), MS4[:MT - 1], 2 * FCH)
        s_zero = sem("acc_zero")
        use_table(ACT.Gelu_apprx_tanh)

        @on("sync")
        def _(e):
            with e.Fori(0, FCH) as ch:
                with e.Fori(0, 4) as j:
                    for slot, w in enumerate(("ffn_w_gate_2", "ffn_w_up_2")):
                        load(e, h0 + 6 * ch + j, slot, t_pieces(slot, T[w][0], D * ch + 256 * j))
                with e.Fori(0, 2) as c:
                    for half in range(2):
                        load(e, h0 + 6 * ch + 4 + c, half, n_pieces(half, T["ffn_w_down_2"][0], KT * ch + 4 * half, 512 * c))

        @on("tensor")
        def _(e):
            e.sem_inc(t2.sem, MT - 1)
            with e.Fori(0, FCH) as ch:
                with e.Fori(0, 4) as j:
                    n = 4 * ch + j
                    gemm_t(e, h0 + 6 * ch + j, 0, hT, (0, 1), [a.before("g", n)])
                    gemm_t(e, h0 + 6 * ch + j, 1, hT, (2, 3), [d.before("m", n)])
                e.wait_ge(*d.at("l", 4 * ch + 3))
                stand(e, s_gate)
                with e.Fori(0, 2) as c:
                    gemm_n(e, h0 + 6 * ch + 4 + c, ff, [4, 5, 6, 7], lambda m: a2.before(f"m{m}", 2 * ch + c), t2)

        @on("scalar")
        def _(e):
            with e.Fori(0, FCH) as ch:
                with e.Fori(0, 4) as j:
                    n, hh = 4 * ch + j, h0 + 6 * ch + j
                    split_hi(e, hh, 1)
                    step(e, a, "g", [used(hh, 0), d.before("c12", n)],
                         lambda: e.activation(padded[:, :, PAD:], pair[0], ACT.Copy))
                    split_hi(e, hh + 1, 0)
                    step(e, a, "e", [d.at("c12", n), d.before("m", n)],
                         lambda: e.activation(tU[:, :, :], tY[:, :, :], ACT.Gelu_apprx_tanh))
                    step(e, a, "h", [d.at("m", n)],
                         lambda: e.activation(ff[0][:, ds(2 * j, 2), :], tZ[:, :, :], ACT.Copy))
                with e.Fori(0, 2) as c:
                    split_hi(e, h0 + 6 * ch + 4 + c, 1)
                    split_hi(e, h0 + 6 * ch + 5 + c, 0)

        @on("vector")
        def _(e):
            e.sem_inc(a2.sem, MT)
            a0 = e.memset(acc[:, :, :], 0.0)
            a0.then_inc(s_zero, 1)
            e.memset(padded[:, :, 0:PAD], 0.0).then_inc(s_zero, 1)
            e.wait_ge(s_zero, 2)
            with e.Fori(0, FCH) as ch:
                with e.Fori(0, 4) as j:
                    n, hh = 4 * ch + j, h0 + 6 * ch + j
                    split_lo(e, hh, 1)
                    for k in range(TAPS):
                        for c in range(2):
                            free = [a.at("g", n), d.before("l", n)] if k == 0 else [d.at(f"c{c}{k - 1}", n)]
                            conv_tap(e, d, n, k, c, 8 * ch + 2 * j + c, G_FCW + 32 * k, G_FCB, free)
                    split_lo(e, hh + 1, 0)
                    step(e, d, "m", [a.at("e", n), used(hh, 1), a.before("h", n)], lambda: e.tensor_tensor(
                        tZ[:, :, :], tU[:, :, :], pair[1], ALU.mult))
                    step(e, d, "l", [a.at("h", n)], lambda: e.tensor_tensor(
                        ff[1][:, ds(2 * j, 2), :], tZ[:, :, :], ff[0][:, ds(2 * j, 2), :].bitcast(F32), ALU.subtract))
                with e.Fori(0, 2) as c:
                    hh = h0 + 6 * ch + 4 + c
                    split_lo(e, hh, 1)
                    split_lo(e, hh + 1, 0)
                    for m in range(MT):
                        to = acc[:, m, ds(512 * c, 512)]
                        step(e, a2, f"m{m}", [n_ready(m, t2, 2 * ch + c, hh), a2.before(f"m{m}", 2 * ch + c)],
                             lambda: e.tensor_tensor(to, to, bank[4 + m], ALU.add))
        H[0] += 6 * FCH
        state["prev"] += [a2]

        a, d, t, _ = phase("out", ["osqrt"], [f"oss{m}" for m in range(MT)] + rstd_dve("o") +
                           [f"{o}{m}" for m in range(MT) for o in "wx"])
        on("sync")(lambda e: load(e, H[0], 0, t_pieces(0, T["w_in"][0], 0)))
        emit_squares("o", d, acc, lambda m: [])
        emit_rstd("o", a, d, d.at(f"oss{MT - 1}"), 1.0 / D, RMS_EPS)

        @on("vector")
        def _(e):
            for m in range(MT):
                step(e, d, f"w{m}", [d.at("on4")], lambda: e.scalar_tensor_tensor(
                    acc[:, m, :], acc[:, m, :], RS[:, m:m + 1], rowB[:, :], ALU.mult, ALU.mult))
                step(e, d, f"x{m}", [d.at(f"w{m}")], lambda: e.tensor_tensor(
                    x_res[:, m, :], x_res[:, m, :], acc[:, m, :], ALU.add))

        @on("sync")
        def _(e):
            for m in range(MT):
                e.wait_ge(*d.at(f"x{m}"))
                e.dma_start(out[0, P * m:P * m + P, :], x_res[:, m, :]).then_inc(s_out, 16)
            e.wait_ge(s_out, 16 * MT)
        program.close()

def constants():
    ratio = np.zeros((P, 4, PAD), np.float32)
    for j, win in enumerate(POOL_WINDOWS):
        ratio[:, j, :] = win / np.minimum(np.arange(1, PAD + 1), win)
    masked = np.float32(-1e30)
    q = np.arange(P)[:, None]
    dist = (S - P + q) - np.arange(S)[None, :]
    causal = np.where(dist >= 0, -dist, masked).astype(np.float32)
    dist = (P + q) - np.arange(2 * P)[None, :]
    banded = np.where((dist >= 0) & (dist < SWA_WINDOW), -dist, masked).astype(np.float32)
    dist = (np.arange(S)[:, None] - (16 * np.arange(N_CMP) + CMP_LEN - 1)[None, :]).reshape(MT, P, N_CMP).transpose(1, 0, 2)
    slopes = np.power(np.float32(2.0), np.arange(1, 17, dtype=np.float32) * np.float32(-0.5))
    slopes = np.concatenate([slopes[m::4] for m in range(4)])
    return {"ident": np.eye(P, dtype=np.float32), "ratio": ratio, "causal": causal, "banded": banded,
            "cmp_dist": np.ascontiguousarray(np.where(dist >= 0, -dist, masked).astype(np.float32)),
            "cmp_mask": np.ascontiguousarray((dist >= 0).astype(np.float32)),
            "slopes": np.ascontiguousarray(np.broadcast_to(slopes, (P, 16)).astype(np.float32))}

def kernel(**inputs):
    import concourse.bacc as bacc
    from concourse.bass_utils import run_bass_kernel_spmd

    nc = bacc.Bacc("TRN2", target_bir_lowering=False, num_devices=1)
    arrays = {n: np.ascontiguousarray(v) for n, v in inputs.items()}
    arrays.update(constants())
    T = {n: nc.dram_tensor(f"in_{n}", v.shape, mybir.dt.from_np(v.dtype), kind="ExternalInput").ap()
         for n, v in arrays.items()}
    out = nc.dram_tensor("out", (1, S, D), F32, kind="ExternalOutput").ap()
    build(nc, T, out)
    r = run_bass_kernel_spmd(nc, [{f"in_{n}": v for n, v in arrays.items()}], core_ids=[0])
    return r.results[0]["out"]
```
